# Optimizing a Trainium2 kernel written in Bass

```python
import math
import jax, jax.numpy as jnp
from jax import lax
import numpy as np

D_MODEL = 1024
BATCH = 1
SEQ = 512
DEPTH = 2
DEC_BATCH = 1
DEC_SEQ = 64
PAST_LEN = 512

CHUNK = 64
PLE_DIM = 256
HEAD_DIM = 64
NORM_EPS = 1e-6
NEG_BIG = -1e30
TINY = 1e-30
Q_BLOCK = 128
D_FF = 2816
MLA_HEADS = 6
MLA_Q_LORA = 256
MLA_KV_LORA = 128
MLA_NOPE = 64
MLA_ROPE = 32
MLA_V = 64
ROPE_BASE = 10000.0
SWA_HEADS = 6
SWA_KV_HEADS = 2
SWA_WINDOW = 128
SWA_WIN_CHUNKS = SWA_WINDOW // CHUNK
HG_HEADS = 4
HG_KEY = 64
HG_VAL = 64
MLA_IN = MLA_Q_LORA + MLA_KV_LORA + MLA_ROPE
SWA_IN = (SWA_HEADS + 2 * SWA_KV_HEADS) * HEAD_DIM
HG_IN = HG_HEADS * (2 * HG_KEY + 2 * HG_VAL)
D_IN = MLA_IN + SWA_IN + HG_IN
D_MIX = MLA_HEADS * MLA_V + SWA_HEADS * HEAD_DIM + HG_HEADS * HG_VAL

kernel_name = 'hybrid_mla_swa_hgrn2_streaming_step'

def rmsnorm(x, g):
    xf = x.astype(jnp.float32)
    y = xf * lax.rsqrt(jnp.mean(xf * xf, axis=-1, keepdims=True) + NORM_EPS)
    return (y * g.astype(jnp.float32)).astype(x.dtype)

def swiglu(u, w_up, w_down):
    gate, val = jnp.split(u @ w_up, 2, axis=-1)
    return (jax.nn.silu(gate) * val) @ w_down

def rope(x, pos):
    half = x.shape[-1] // 2
    inv = jnp.exp(-math.log(ROPE_BASE) * jnp.arange(half, dtype=jnp.float32) / half)
    ang = pos.astype(jnp.float32)[:, None] * inv[None, :]
    cos = jnp.cos(ang)[None, :, None, :]
    sin = jnp.sin(ang)[None, :, None, :]
    xf = x.astype(jnp.float32)
    x1, x2 = xf[..., :half], xf[..., half:]
    return jnp.concatenate([x1 * cos - x2 * sin, x2 * cos + x1 * sin], axis=-1).astype(x.dtype)

def alibi_slopes(n):
    return jnp.exp2(-8.0 * jnp.arange(1, n + 1, dtype=jnp.float32) / n)

def mla_attend(q_nope, q_rope, ckv_all, krope_all, q_pos, k_pos, w_ukv):
    B, Tq, H, _ = q_nope.shape
    w = w_ukv.reshape(MLA_KV_LORA, H, MLA_NOPE + MLA_V)
    w_uk, w_uv = w[..., :MLA_NOPE], w[..., MLA_NOPE:]
    q_lat = jnp.einsum('bthn,chn->bthc', q_nope, w_uk)
    scale = (MLA_NOPE + MLA_ROPE) ** -0.5
    qb = Q_BLOCK if Tq % Q_BLOCK == 0 else Tq
    nb = Tq // qb
    k_chunk = k_pos // CHUNK

    def block(args):
        ql, qr, qp = args
        s = jnp.einsum('bqhc,bkc->bhqk', ql, ckv_all) + jnp.einsum('bqhr,bkr->bhqk', qr, krope_all)
        s = s.astype(jnp.float32) * scale
        vis = k_chunk[None, :] <= (qp // CHUNK)[:, None]
        p = jax.nn.softmax(jnp.where(vis, s, NEG_BIG), axis=-1)
        return jnp.einsum('bhqk,bkc->bqhc', p.astype(ckv_all.dtype), ckv_all)

    to_blocks = lambda t: jnp.moveaxis(t.reshape(B, nb, qb, *t.shape[2:]), 1, 0)
    o_lat = lax.map(block, (to_blocks(q_lat), to_blocks(q_rope), q_pos.reshape(nb, qb)))
    o_lat = jnp.moveaxis(o_lat, 0, 1).reshape(B, Tq, H, MLA_KV_LORA)
    return jnp.einsum('bthc,chv->bthv', o_lat, w_uv).reshape(B, Tq, H * MLA_V)

def mla_mixer(a, pos, past, q_norm, w_uq, kv_norm, w_ukv):
    B, T, _ = a.shape
    c_q, c_kv, k_r = jnp.split(a, [MLA_Q_LORA, MLA_Q_LORA + MLA_KV_LORA], axis=-1)
    q = (rmsnorm(c_q, q_norm) @ w_uq).reshape(B, T, MLA_HEADS, MLA_NOPE + MLA_ROPE)
    q_nope, q_rope = q[..., :MLA_NOPE], rope(q[..., MLA_NOPE:], pos)
    ckv = rmsnorm(c_kv, kv_norm)
    krope = rope(k_r[:, :, None, :], pos)[:, :, 0, :]
    if past is None:
        ckv_all, krope_all, k_pos = ckv, krope, pos
    else:
        ckv_all = jnp.concatenate([past[0], ckv], axis=1)
        krope_all = jnp.concatenate([past[1], krope], axis=1)
        k_pos = jnp.arange(past[0].shape[1] + T, dtype=jnp.int32)
    out = mla_attend(q_nope, q_rope, ckv_all, krope_all, pos, k_pos, w_ukv)
    return out, (ckv, krope)

def sink_attend(q, k, v, q_pos, k_pos, sinks):
    *lead, Tq, H, D = q.shape
    kvh = k.shape[-2]
    g = H // kvh
    qg = q.reshape(*lead, Tq, kvh, g, D)
    s = jnp.einsum('...qhgd,...shd->...hgqs', qg, k).astype(jnp.float32) * (D ** -0.5)
    dist = jnp.abs(q_pos[..., :, None] - k_pos[..., None, :]).astype(jnp.float32)
    qc, kc = q_pos // CHUNK, k_pos // CHUNK
    vis = ((k_pos[..., None, :] >= 0) & (kc[..., None, :] <= qc[..., :, None])
           & (kc[..., None, :] >= qc[..., :, None] - SWA_WIN_CHUNKS))
    s = s - alibi_slopes(H).reshape(kvh, g, 1, 1) * dist[..., None, None, :, :]
    s = jnp.where(vis[..., None, None, :, :], s, NEG_BIG)
    sink = sinks.astype(jnp.float32).reshape(kvh, g, 1, 1)
    m = jnp.maximum(jnp.max(s, axis=-1, keepdims=True), sink)
    e = jnp.exp(s - m)
    p = e / (jnp.sum(e, axis=-1, keepdims=True) + jnp.exp(sink - m))
    o = jnp.einsum('...hgqs,...shd->...qhgd', p.astype(v.dtype), v)
    return o.reshape(*lead, Tq, H * D)

def swa_mixer(a, pos, past, sinks):
    B, T, _ = a.shape
    q, k, v = jnp.split(a, [SWA_HEADS * HEAD_DIM, (SWA_HEADS + SWA_KV_HEADS) * HEAD_DIM], axis=-1)
    q = q.reshape(B, T, SWA_HEADS, HEAD_DIM)
    k = k.reshape(B, T, SWA_KV_HEADS, HEAD_DIM)
    v = v.reshape(B, T, SWA_KV_HEADS, HEAD_DIM)
    if past is None:
        nc = T // CHUNK
        qc = q.reshape(B, nc, CHUNK, SWA_HEADS, HEAD_DIM)

        def band(t):
            tc = t.reshape(B, nc, CHUNK, SWA_KV_HEADS, HEAD_DIM)
            tp = jnp.pad(tc, ((0, 0), (SWA_WIN_CHUNKS, 0), (0, 0), (0, 0), (0, 0)))
            return jnp.concatenate([tp[:, j:j + nc] for j in range(SWA_WIN_CHUNKS + 1)], axis=2)

        q_pos = pos.reshape(nc, CHUNK)
        k_pos = ((jnp.arange(nc, dtype=jnp.int32)[:, None] - SWA_WIN_CHUNKS) * CHUNK
                 + jnp.arange((SWA_WIN_CHUNKS + 1) * CHUNK, dtype=jnp.int32)[None, :])
        o = sink_attend(qc, band(k), band(v), q_pos, k_pos, sinks).reshape(B, T, SWA_HEADS * HEAD_DIM)
        new = (k[:, -SWA_WINDOW:], v[:, -SWA_WINDOW:])
    else:
        w = past[0].shape[1]
        k_all = jnp.concatenate([past[0], k], axis=1)
        v_all = jnp.concatenate([past[1], v], axis=1)
        k_pos = pos[0] - w + jnp.arange(w + T, dtype=jnp.int32)
        o = sink_attend(q, k_all, v_all, pos, k_pos, sinks)
        new = (k_all[:, -SWA_WINDOW:], v_all[:, -SWA_WINDOW:])
    return o, new

def hgrn2_chunkwise(q, k, v, logf, s0):
    B, L = q.shape[0], q.shape[1]
    c = CHUNK if L % CHUNK == 0 else L
    n = L // c
    to_chunks = lambda t: jnp.swapaxes(t.reshape(B, n, c, *t.shape[2:]), 0, 1)
    tri = jnp.tril(jnp.ones((c, c), dtype=bool))[None, :, :, None, None]

    def step(S, inp):
        qc, kc, vc, gc = inp
        G = jnp.cumsum(gc, axis=1)
        o_inter = jnp.einsum('bthk,bhkv->bthv', qc * jnp.exp(G), S)
        diff = G[:, :, None] - G[:, None, :]
        decay = jnp.exp(jnp.where(tri, diff, NEG_BIG))
        A = jnp.einsum('bthk,bshk,btshk->bhts', qc, kc, decay)
        o_intra = jnp.einsum('bhts,bshv->bthv', A, vc)
        GT = G[:, -1]
        k_dec = kc * jnp.exp(GT[:, None] - G)
        S_new = jnp.exp(GT)[..., None] * S + jnp.einsum('bshk,bshv->bhkv', k_dec, vc)
        return S_new, o_inter + o_intra

    s_fin, o = lax.scan(step, s0, (to_chunks(q), to_chunks(k), to_chunks(v), to_chunks(logf)))
    return jnp.swapaxes(o, 0, 1).reshape(B, L, *v.shape[2:]), s_fin

def hgrn2_mixer(a, lb, past, out_norm):
    B, T, _ = a.shape
    hk, hv = HG_HEADS * HG_KEY, HG_HEADS * HG_VAL
    q, f, i, g = jnp.split(a, [hk, 2 * hk, 2 * hk + hv], axis=-1)
    q = jax.nn.silu(q.astype(jnp.float32)).reshape(B, T, HG_HEADS, HG_KEY) * (HG_KEY ** -0.5)
    lbf = lb.astype(jnp.float32)
    fgate = lbf + (1.0 - lbf) * jax.nn.sigmoid(f.astype(jnp.float32))
    logf = jnp.log(jnp.maximum(fgate, TINY)).reshape(B, T, HG_HEADS, HG_KEY)
    k = (1.0 - fgate).reshape(B, T, HG_HEADS, HG_KEY)
    v = i.astype(jnp.float32).reshape(B, T, HG_HEADS, HG_VAL)
    if past is None:
        s0 = jnp.zeros((B, HG_HEADS, HG_KEY, HG_VAL), jnp.float32)
    else:
        s0 = past.astype(jnp.float32)
    o, s_fin = hgrn2_chunkwise(q, k, v, logf, s0)
    o = rmsnorm(o, out_norm) * jax.nn.silu(g.astype(jnp.float32).reshape(B, T, HG_HEADS, HG_VAL))
    return o.reshape(B, T, hv).astype(a.dtype), s_fin.astype(a.dtype)

def layer_forward(x, p_i, pos, past, w, lb):
    h = x + 0.5 * swiglu(rmsnorm(x, w['ffn1_norm']), w['ffn1_up'], w['ffn1_down'])
    a = rmsnorm(h, w['mix_norm']) @ w['w_in']
    a_mla, a_swa, a_hg = jnp.split(a, [MLA_IN, MLA_IN + SWA_IN], axis=-1)
    if past is None:
        p_mla, p_swa, p_hg = None, None, None
    else:
        p_mla, p_swa, p_hg = (past[0], past[1]), (past[2], past[3]), past[4]
    o_mla, (ckv, krope) = mla_mixer(a_mla, pos, p_mla, w['mla_q_norm'], w['mla_w_uq'],
                                    w['mla_kv_norm'], w['mla_w_ukv'])
    o_swa, (sk, sv) = swa_mixer(a_swa, pos, p_swa, w['swa_sinks'])
    o_hg, s_hg = hgrn2_mixer(a_hg, lb, p_hg, w['hg_out_norm'])
    h = h + jnp.concatenate([o_mla, o_swa, o_hg], axis=-1) @ w['w_out']
    h = h + 0.5 * swiglu(rmsnorm(h, w['ffn2_norm']), w['ffn2_up'], w['ffn2_down'])
    gate = jax.nn.sigmoid(rmsnorm(h, w['ple_norm']) @ w['ple_gate'])
    h = h + gate * (p_i @ w['ple_proj'])
    return h, (ckv, krope, sk, sv, s_hg)

def setup_inputs(seed: int = 0) -> dict:
    key = jax.random.key(seed)
    ks = jax.random.split(key, 40)
    it = iter([ks[j] for j in range(40)])
    nrm = lambda shape, scale: jax.random.normal(next(it), shape, jnp.float32) * scale
    gain = lambda shape: 1.0 + 0.05 * jax.random.normal(next(it), shape, jnp.float32)
    return {
        'x_prompt': nrm((BATCH, SEQ, D_MODEL), 1.0),
        'x_sample': nrm((DEC_BATCH, DEC_SEQ, D_MODEL), 1.0),
        'p_prompt': nrm((DEPTH, BATCH, SEQ, PLE_DIM), 1.0),
        'p_sample': nrm((DEPTH, DEC_BATCH, DEC_SEQ, PLE_DIM), 1.0),
        'cache_mla_ckv': nrm((DEPTH, DEC_BATCH, PAST_LEN, MLA_KV_LORA), 1.0),
        'cache_mla_krope': nrm((DEPTH, DEC_BATCH, PAST_LEN, MLA_ROPE), 1.0),
        'cache_swa_k': nrm((DEPTH, DEC_BATCH, SWA_WINDOW, SWA_KV_HEADS, HEAD_DIM), 1.0),
        'cache_swa_v': nrm((DEPTH, DEC_BATCH, SWA_WINDOW, SWA_KV_HEADS, HEAD_DIM), 1.0),
        'state_hgrn': nrm((DEPTH, DEC_BATCH, HG_HEADS, HG_KEY, HG_VAL), 0.5),
        'ffn1_norm': gain((DEPTH, D_MODEL)),
        'ffn1_up': nrm((DEPTH, D_MODEL, 2 * D_FF), D_MODEL ** -0.5),
        'ffn1_down': nrm((DEPTH, D_FF, D_MODEL), D_FF ** -0.5),
        'mix_norm': gain((DEPTH, D_MODEL)),
        'w_in': nrm((DEPTH, D_MODEL, D_IN), D_MODEL ** -0.5),
        'mla_q_norm': gain((DEPTH, MLA_Q_LORA)),
        'mla_w_uq': nrm((DEPTH, MLA_Q_LORA, MLA_HEADS * (MLA_NOPE + MLA_ROPE)), MLA_Q_LORA ** -0.5),
        'mla_kv_norm': gain((DEPTH, MLA_KV_LORA)),
        'mla_w_ukv': nrm((DEPTH, MLA_KV_LORA, MLA_HEADS * (MLA_NOPE + MLA_V)), MLA_KV_LORA ** -0.5),
        'swa_sinks': nrm((DEPTH, SWA_HEADS), 0.5),
        'hg_lb_logits': nrm((DEPTH, HG_HEADS * HG_KEY), 0.5),
        'hg_out_norm': gain((DEPTH, HG_VAL)),
        'w_out': nrm((DEPTH, D_MIX, D_MODEL), D_MIX ** -0.5),
        'ffn2_norm': gain((DEPTH, D_MODEL)),
        'ffn2_up': nrm((DEPTH, D_MODEL, 2 * D_FF), D_MODEL ** -0.5),
        'ffn2_down': nrm((DEPTH, D_FF, D_MODEL), D_FF ** -0.5),
        'ple_norm': gain((DEPTH, D_MODEL)),
        'ple_gate': nrm((DEPTH, D_MODEL, D_MODEL), D_MODEL ** -0.5),
        'ple_proj': nrm((DEPTH, PLE_DIM, D_MODEL), PLE_DIM ** -0.5),
        'final_norm': gain((D_MODEL,)),
    }

def reference(x_prompt, x_sample, p_prompt, p_sample, cache_mla_ckv, cache_mla_krope, cache_swa_k,
              cache_swa_v, state_hgrn, ffn1_norm, ffn1_up, ffn1_down, mix_norm, w_in, mla_q_norm,
              mla_w_uq, mla_kv_norm, mla_w_ukv, swa_sinks, hg_lb_logits, hg_out_norm, w_out,
              ffn2_norm, ffn2_up, ffn2_down, ple_norm, ple_gate, ple_proj, final_norm):
    lb_sm = jax.nn.softmax(hg_lb_logits.astype(jnp.float32), axis=0)
    lb_all = jnp.cumsum(lb_sm, axis=0) - lb_sm[0]
    layers = [dict(ffn1_norm=ffn1_norm[i], ffn1_up=ffn1_up[i], ffn1_down=ffn1_down[i], mix_norm=mix_norm[i],
                   w_in=w_in[i], mla_q_norm=mla_q_norm[i], mla_w_uq=mla_w_uq[i], mla_kv_norm=mla_kv_norm[i],
                   mla_w_ukv=mla_w_ukv[i], swa_sinks=swa_sinks[i], hg_out_norm=hg_out_norm[i],
                   w_out=w_out[i], ffn2_norm=ffn2_norm[i], ffn2_up=ffn2_up[i], ffn2_down=ffn2_down[i],
                   ple_norm=ple_norm[i], ple_gate=ple_gate[i], ple_proj=ple_proj[i])
              for i in range(DEPTH)]
    past_len = cache_mla_ckv.shape[2]
    pos_prompt = jnp.arange(x_prompt.shape[1], dtype=jnp.int32)
    pos_sample = past_len + jnp.arange(x_sample.shape[1], dtype=jnp.int32)
    hp, hs = x_prompt, x_sample
    st_p, st_s = [], []
    for i in range(DEPTH):
        hp, sp = layer_forward(hp, p_prompt[i], pos_prompt, None, layers[i], lb_all[i])
        past = (cache_mla_ckv[i], cache_mla_krope[i], cache_swa_k[i], cache_swa_v[i], state_hgrn[i])
        hs, ss = layer_forward(hs, p_sample[i], pos_sample, past, layers[i], lb_all[i])
        st_p.append(sp)
        st_s.append(ss)
    y_prompt = rmsnorm(hp, final_norm)
    y_sample = rmsnorm(hs, final_norm)
    stack = lambda sts, j: jnp.stack([s[j] for s in sts], axis=0)
    new_ckv_prompt = stack(st_p, 0)
    new_krope_prompt = stack(st_p, 1)
    new_swa_k_prompt = stack(st_p, 2)
    new_swa_v_prompt = stack(st_p, 3)
    new_hgrn_prompt = stack(st_p, 4)
    new_ckv_sample = stack(st_s, 0)
    new_krope_sample = stack(st_s, 1)
    new_swa_k_sample = stack(st_s, 2)
    new_swa_v_sample = stack(st_s, 3)
    new_hgrn_sample = stack(st_s, 4)
    return (y_prompt, y_sample, new_ckv_prompt, new_krope_prompt, new_swa_k_prompt, new_swa_v_prompt,
            new_hgrn_prompt, new_ckv_sample, new_krope_sample, new_swa_k_sample, new_swa_v_sample,
            new_hgrn_sample)


_drawn_inputs = setup_inputs


def setup_inputs(seed=0):
    import zlib

    import numpy as np

    out = dict(_drawn_inputs(seed))
    spreads = {}
    factors = {'mla_q_norm': 8.0, 'swa_sinks': 8.0, 'hg_out_norm': 3.408, 'ple_norm': 4.861}
    for name, (base, spread) in spreads.items():
        noise = np.random.default_rng([zlib.crc32(name.encode()), seed]).standard_normal(out[name].shape)
        drawn = base * np.exp(spread * noise) if base else spread * noise
        out[name] = __import__('jax').numpy.asarray(drawn.astype(out[name].dtype))
    for name, factor in factors.items():
        out[name] = (out[name] * factor).astype(out[name].dtype)
    return out
```

```python
from contextlib import ExitStack

import numpy as np

import concourse.bass as bass
from concourse import mybir

F32 = mybir.dt.float32
F32R = mybir.dt.float32r
U8 = mybir.dt.uint8
ALU = mybir.AluOpType
ACT = mybir.ActivationFunctionType
AX = mybir.AxisListType

P = 128
DEPTH, D_MODEL, D_FF = 2, 1024, 2816
PROMPT, SAMPLE, PAST = 512, 64, 512
TOK = PROMPT + SAMPLE
HALF = TOK // 2
KD = D_MODEL // P
EPS, TINY = 1e-6, 1e-30
CHUNK_W = KD * P
FF_GROUPS = (8, 8, 6)
ROPE, NOPE = 32, 64
MLA_SCALE = (NOPE + ROPE) ** -0.5
SWA_SCALE = 64 ** -0.5
NEG = -1e30
FAR = 1e33
W_SLOTS, RAW_SLOTS, AHEAD = 4, 2, 3
LEVELS = 8
BLOCKS = ((0, 128), (128, 128), (256, 128), (384, 128), (512, 64))

W_IN = ("f0", "f1", "q0", "q1", "g0", "g1", "i0", "i1", "ckv", "kr", "cq0", "cq1", "swk", "swv",
        "swq0", "swq1", "swq2", "spare")
PAR = dict(mix=0, ffn2=8, ple=16, next=24, q_norm=32, kv_norm=34, hg_out=35, sink=36)
PAR_W = 42


def plan():
    chunks, uses, last_use = {}, {}, []

    def use(name):
        uses[name] = len(uses)

    def chunk(name, *made):
        chunks[name] = len(chunks)
        for m in made or (name,):
            use(m)
        last_use.append(len(uses) - 1)

    def ffn(f):
        for g, pairs in enumerate(FF_GROUPS):
            for q in range(2 * pairs):
                chunk(f"{f}.{g}.up{q}")
                if g == 0 and q == 1:
                    use(f"{f}.norm")
            for m in range(KD):
                chunk(f"{f}.{g}.down{m}")

    ffn("ffn1")
    for name in W_IN:
        if name == "spare":
            chunks[name] = len(chunks)
            last_use.append(len(uses) - 1)
            continue
        chunk(name)
        if name == "f1":
            use("mix.norm")
        if name == "cq1":
            use("ckv.norm")
        if name == "swk":
            use("kr.sum")
            use("cq.norm")
    for m in range(KD):
        chunk(f"out{m}")
    ffn("ffn2")
    for half in range(2):
        chunk(f"proj{half}", *(f"proj{half}.{m}" for m in range(4)))
        for m in range(4):
            chunk(f"gate{4 * half + m}")
            if half == 0 and m == 0:
                use("ple.norm")
    assert len(chunks) % W_SLOTS == 0
    return chunks, uses, last_use


CH, US, LAST = plan()
N_CH = len(CH)
PAD_US = -len(US) % 4
N_US = len(US) + PAD_US


UNIT_Q = (P, P, P, P, SAMPLE)

def unit_keys(kind, b):
    if kind == "swa":
        return (128, 256, 256, 256, 192)[b]
    return (128, 256, 384, 512, PAST + SAMPLE)[b]

def unit_tiles(kind, b):
    if kind == "swa":
        return ((0,), (0, 1), (1, 2), (2, 3), (4, 5))[b]
    return ((0,), (0, 1), (0, 1, 2), (0, 1, 2, 3), (4, 5, 6, 7, 8))[b]


class Event:

    def __init__(self, ctx, nc, name, per, seed=0):
        self.sem = ctx.enter_context(nc.semaphore(name))
        self.per, self.seed = per, seed

    def at(self, layer, count, more=0):
        return layer * self.per + (count + self.seed) + more


def hybrid_step(nc, x_t, p_t, w_all, uq, ukv, par_d, logits_d, cos_sin, ident_d, ones_d, head_ones_d, comb_d,
                dist_d, mask_d, late_d, ckv_c, krope_c, swk_c, swv_c, hg_s,
                y_t, ckv_o, krope_o, swk_o, swv_o, hg_o):
    ctx = ExitStack()
    with ctx:
        base = -(-nc.sbuf_base // 64) * 64
        top = [base]

        def place(name, shape, dt=F32, at=None):
            size = int(np.prod(shape[1:])) * (1 if dt == U8 else 4)
            offset = top[0] if at is None else at
            if at is None:
                top[0] += -(-size // 32) * 32
            return nc.alloc_sbuf_tensor_at(name, shape, dt, offset=offset)

        T_BYTES = TOK * 4
        h = place("h", [P, KD, TOK])
        xg_at = top[0]
        xg_hi = place("xg_hi", [P, KD, TOK], F32R)
        xg_lo = place("xg_lo", [P, KD, TOK], F32R)
        xg_end = top[0]
        hid_at = top[0]
        hid_hi = place("hid_hi", [P, KD, TOK], F32R)
        hid_lo_at = top[0]
        hid_lo = place("hid_lo", [P, KD, TOK], F32R)
        w_raw = place("w_raw", [P, RAW_SLOTS, CHUNK_W])
        w_hi = place("w_hi", [P, W_SLOTS, CHUNK_W], F32R)
        w_lo = place("w_lo", [P, W_SLOTS, CHUNK_W], F32R)
        r = place("r", [P, TOK])
        r_col = place("r_col", [P, 5])
        acc = place("acc", [P, TOK])
        sq = place("sq", [P, TOK])
        par = place("par", [P, PAR_W])
        cs = place("cs", [P, TOK])
        ident = place("ident", [P, P])
        ones = place("ones", [P, P])
        head_ones = place("head_ones", [P, P])
        comb = place("comb", [P, 3, 96])
        dist = place("dist", [P, 256])
        mask = place("mask", [P, LEVELS - 1, P], U8)
        late = place("late", [1, P + 64])
        eps = place("eps", [P, 1])
        lbl = place("lbl", [P, DEPTH, 2])
        lbt = place("lbt", [P, 4, 2])
        lb = place("lb", [P, 2])
        lb_next = place("lb_next", [P, 2])
        one_minus_lb = place("one_minus_lb", [P, 2])
        no_sink = place("no_sink", [P, 6])
        p_raw = place("p_raw", [P, 2, TOK])
        dense_at = top[0]
        G = place("G", [P, 2, TOK])
        hk = place("hk", [P, 2, TOK])
        hq = place("hq", [P, 2, TOK])
        hg = place("hg", [P, 2, TOK])
        gate = place("gate", [P, 2, TOK], at=dense_at)
        val = place("val", [P, 2, TOK], at=dense_at + 2 * T_BYTES)
        p_hi = place("p_hi", [P, 2, TOK], F32R, at=dense_at + 4 * T_BYTES)
        p_lo = place("p_lo", [P, 2, TOK], F32R, at=dense_at + 6 * T_BYTES)
        V = place("V", [P, 5, 256])
        S = place("S", [P, 2, 7, 64])
        a_tail = place("a_tail", [64, 2, 64])
        e_end = place("e_end", [P, 2, 5])
        swq = place("swq", [P, 3, TOK])
        swk = place("swk", [P, PROMPT + 128 + SAMPLE])
        swv = place("swv", [P, 6, P])
        cq = place("cq", [P, 2, TOK])
        ckv = place("ckv", [P, PROMPT + PAST + SAMPLE])
        krs = place("krs", [P, TOK])
        uq_w = place("uq_w", [P, 2, 3, 256])
        assert top[0] <= nc.sbuf_usable_end, (top[0], nc.sbuf_usable_end)
        tmp = place("tmp", [P, 6, TOK], at=hid_at)
        mask_f = place("mask_f", [P, LEVELS - 1, P], at=hid_at)
        qG = place("qG", [P, 2, TOK], at=hid_lo_at)
        kdT = place("kdT", [P, 2, 5, P], at=hid_lo_at + 2 * T_BYTES)
        fx = place("fx", [P, 2, TOK], at=hid_lo_at + 2 * T_BYTES)
        A = place("A", [P, 2, 4, P], at=hid_lo_at + 2 * T_BYTES + 5120)
        pp = place("pp", [P, 4, TOK], at=hid_at)
        y = place("y", [P, KD, TOK], at=hid_at)
        off = [xg_at]

        def over(name, shape):
            t = place(name, shape, at=off[0])
            off[0] += -(-int(np.prod(shape[1:])) * 4 // 32) * 32
            assert off[0] <= xg_end
            return t

        kT = [over(f"kT{a}", [P, PROMPT + PAST + SAMPLE]) for a in range(2)]
        qT = [over(f"qT{a}", [P, TOK]) for a in range(2)]
        mv = over("mv", [P, 9, P])
        tq = over("tq", [P, TOK])
        prob = over("prob", [P, 2, TOK])
        probT = over("probT", [P, 2, PROMPT])
        score = over("score", [P, 2, 256])
        stat = over("stat", [P, 2, 6])
        ukv_w = over("ukv_w", [P, 3, 256])

        ps = ctx.enter_context(nc.psum_tensor("ps", [P, 8, 512], F32))

        def slot(u):
            return ps[:, 2 * (u % 4):2 * (u % 4) + 2, 0:HALF]

        def bank(u):
            return 2 * (u % 4)

        def halves(ap):
            return ap.rearrange("p (a n) -> p a n", a=2)

        def ev(name, per, seed=0):
            return Event(ctx, nc, name, per, seed)

        raw_in = [ev(f"raw_in{s}", 16 * N_CH // RAW_SLOTS) for s in range(RAW_SLOTS)]
        whi_ready = ev("whi_ready", N_CH)
        wlo_ready = ev("wlo_ready", N_CH, RAW_SLOTS)
        made = ev("made", N_US, 8)
        drained = ev("drained", N_US, 4)
        silu_done = ev("silu_done", 44)
        prod_done = ev("prod_done", 44)
        hidhi_ready = ev("hidhi_ready", 44)
        hid_ready = ev("hid_ready", 44)
        xhi_ready = ev("xhi_ready", 32, 8)
        xg_ready = ev("xg_ready", 32, 8)
        sq_done = ev("sq_done", 28, 7)
        acc_done = ev("acc_done", 32, 8)
        root_done = ev("root_done", 7)
        inverted = ev("inverted", 4)
        passed = ev("passed", 0)
        const_in = ev("const_in", 0)
        x_in = ev("x_in", 0)
        set_up = ev("set_up", 0)
        lb_step = ev("lb_step", 0)
        lb_exp = ev("lb_exp", 0)
        layer_in = ev("layer_in", 16 * 7)
        late_in = ev("late_in", 16 * 3)
        silu_in = ev("silu_in", 2)
        c_raw = ev("c_raw", 1)
        c_sq = ev("c_sq", 3)
        c_norm = ev("c_norm", 7)
        f_exp = ev("f_exp", 1)
        f_step = ev("f_step", 8)
        f_ln = ev("f_ln", 1)
        G_ready = ev("G_ready", 10)
        eG_ready = ev("eG_ready", 1)
        qG_ready = ev("qG_ready", 3)
        kd_diff = ev("kd_diff", 3)
        kd_exp = ev("kd_exp", 1)
        kd_ready = ev("kd_ready", 1)
        kd_turned = ev("kd_turned", 1)
        kdT_ready = ev("kdT_ready", 4)
        dS_made = ev("dS_made", 1)
        S_ready = ev("S_ready", 10)
        lv_diff = ev("lv_diff", 28)
        lv_exp = ev("lv_exp", 14)
        lv_qk = ev("lv_qk", 28)
        A_made = ev("A_made", 16)
        tail_made = ev("tail_made", 14)
        tail_out = ev("tail_out", 2)
        A_taken = ev("A_taken", 32)
        O_made = ev("O_made", 2)
        O_out = ev("O_out", 4)
        O_sq = ev("O_sq", 1)
        O_ms = ev("O_ms", 1)
        O_root = ev("O_root", 2)
        O_norm = ev("O_norm", 3)
        O_hi = ev("O_hi", 1)
        O_lo = ev("O_lo", 1)
        k_placed = ev("k_placed", 4)
        s_made = [ev(f"s_made{i}", 39) for i in range(2)]
        s_free = [ev(f"s_free{i}", 39, 1) for i in range(2)]
        scored = ev("scored", 60)
        bound_done = ev("bound_done", 60)
        exp_done = ev("exp_done", 60)
        sink_done = ev("sink_done", 30)
        den_done = ev("den_done", 30)
        recip_done = ev("recip_done", 30)
        prob_ready = ev("prob_ready", 60)
        turned = ev("turned", 60)
        probT_ready = ev("probT_ready", 60)
        pv_done = ev("pv_done", 60)
        att_hi = ev("att_hi", 12)
        att_lo = ev("att_lo", 12)
        p_split = ev("p_split", 1)
        p_ready = ev("p_ready", 1)
        sig_done = ev("sig_done", 8)
        emb_mul = ev("emb_mul", 8)
        h_emb = ev("h_emb", 8)
        y_done = ev("y_done", 0)
        stored = ev("stored", 16 * 10)

        block = ctx.enter_context(nc.Block())

        def by_itself(engine):
            engine.sem_inc(passed.sem, 1)

        UP = [(f, g, pairs) for f in ("ffn1", "ffn2") for g, pairs in enumerate(FF_GROUPS)]

        def hid_before(f, g):
            return sum(FF_GROUPS[:g]) + (22 if f == "ffn2" else 0)

        @block.sync
        def _(sp):
            def load(layer, n, count):
                assert n % RAW_SLOTS == 0 and count % RAW_SLOTS == 0
                with sp.Fori(0, count // RAW_SLOTS) as i:
                    for s in range(RAW_SLOTS):
                        sp.wait_ge(wlo_ready.sem, layer * N_CH + (n + s + 1) + i * RAW_SLOTS)
                        sp.dma_start(w_raw[:, s, :], w_all[layer * N_CH + (n + s) + i * RAW_SLOTS]) \
                          .then_inc(raw_in[s].sem, 16)

            with sp.Fori(0, DEPTH) as L:
                load(L, 0, 16)
                sp.wait_ge(xg_ready.sem, xg_ready.at(L, 0))
                sp.dma_start(par[:, :], par_d[L]).then_inc(layer_in.sem, 16)
                sp.dma_start(uq_w[:, :, :, :], uq[L]).then_inc(layer_in.sem, 16)
                sp.dma_start(ckv[:, PROMPT:PROMPT + PAST], ckv_c[L]).then_inc(layer_in.sem, 16)
                sp.dma_start(swk[:, PROMPT:PROMPT + 128], swk_c[L]).then_inc(layer_in.sem, 16)
                sp.dma_start(swv[:, 4, :], swv_c[L]).then_inc(layer_in.sem, 16)
                sp.dma_start(S[:, :, 5, :], hg_s[L]).then_inc(layer_in.sem, 16)
                sp.dma_start(p_raw[:, :, :], p_t[L]).then_inc(layer_in.sem, 16)
                n_mix = CH["out2"] + 1 + (CH["out2"] + 1) % 2
                load(L, 16, n_mix - 16)
                sp.wait_ge(made.sem, made.at(L, US["swq2"] + 1))
                sp.dma_start(kT[0][64:96, PROMPT:PROMPT + PAST], krope_c[L]).then_inc(late_in.sem, 16)
                sp.dma_start(kT[1][64:96, PROMPT:PROMPT + PAST], krope_c[L]).then_inc(late_in.sem, 16)
                sp.dma_start(ukv_w[:, :, :], ukv[L]).then_inc(late_in.sem, 16)
                sp.wait_ge(c_norm.sem, c_norm.at(L, 7))
                sp.dma_start(ckv_o[L, :, 0:PROMPT], ckv[:, 0:PROMPT]).then_inc(stored.sem, 16)
                sp.dma_start(ckv_o[L, :, PROMPT:TOK], ckv[:, PROMPT + PAST:]).then_inc(stored.sem, 16)
                sp.dma_start(krope_o[L], krs[64:96, :]).then_inc(stored.sem, 16)
                sp.wait_ge(drained.sem, drained.at(L, US["swq2"] + 1))
                sp.dma_start(swk_o[L, 0], swk[:, PROMPT - 128:PROMPT]).then_inc(stored.sem, 16)
                sp.dma_start(swk_o[L, 1], swk[:, PROMPT + 64:]).then_inc(stored.sem, 16)
                sp.dma_start(swv_o[L, 0], swv[:, 3, :]).then_inc(stored.sem, 16)
                sp.dma_start(swv_o[L, 1, 0:64], swv[64:128, 4, :]).then_inc(stored.sem, 16)
                sp.dma_start(swv_o[L, 1, 64:128], swv[0:64, 5, :]).then_inc(stored.sem, 16)
                sp.wait_ge(S_ready.sem, S_ready.at(L, 10))
                sp.dma_start(hg_o[L, 0], S[:, :, 4, :]).then_inc(stored.sem, 16)
                sp.dma_start(hg_o[L, 1], S[:, :, 6, :]).then_inc(stored.sem, 16)
                sp.wait_ge(stored.sem, stored.at(L, stored.per))
                by_itself(sp)
                load(L, n_mix, N_CH - n_mix)
            for n in range(AHEAD):
                sp.wait_ge(wlo_ready.sem, DEPTH * N_CH + n + 1)
                sp.dma_start(w_raw[:, n % RAW_SLOTS, :], w_all[DEPTH * N_CH + n]) \
                  .then_inc(raw_in[n % RAW_SLOTS].sem, 16)
            for t in range(KD):
                sp.wait_ge(y_done.sem, t + 1)
                sp.dma_start(y_t[:, t, :], y[:, t, :]).then_inc(stored.sem, 16)
            sp.wait_ge(stored.sem, DEPTH * stored.per + 16 * KD)

        @block.scalar
        def _(act):
            act.dma_start(h[:, :, :], x_t).then_inc(x_in.sem, 16)
            act.dma_start(par[:, :], par_d[DEPTH]).then_inc(x_in.sem, 16)
            for dst, src in ((cs[:, :], cos_sin), (ident[:, :], ident_d), (ones[:, :], ones_d),
                             (head_ones[:, :], head_ones_d), (comb[:, :, :], comb_d), (dist[:, :], dist_d),
                             (mask_f[:, :, :], mask_d), (late[:, :], late_d), (lbl[:, :, :], logits_d)):
                act.dma_start(dst, src).then_inc(const_in.sem, 16)

            def split_hi(layer, n, more=0):
                s = n % W_SLOTS
                act.wait_ge(raw_in[n % RAW_SLOTS].sem,
                            layer * raw_in[0].per + 16 * (n // RAW_SLOTS + 1) + more * (16 * 4 // RAW_SLOTS))
                free = LAST[n - 4] + 1 if n >= 4 else LAST[N_CH + n - 4] + 1 - len(US) - PAD_US
                act.wait_ge(made.sem, layer * N_US + (free + made.seed) + more * 4)
                act.activation(w_hi[:, s, :], w_raw[:, n % RAW_SLOTS, :], ACT.Copy).then_inc(whi_ready.sem, 1)

            def step(layer, n, more=0):
                split_hi(layer, n + AHEAD, more) if n + AHEAD < N_CH else split_hi(layer + 1, n + AHEAD - N_CH, more)

            def root(layer, use, scale, out, k):
                act.wait_ge(made.sem, made.at(layer, US[use] + 1))
                act.activation(halves(out), slot(US[use]), ACT.Sqrt, bias=eps[:, 0:1], scale=scale) \
                   .then_inc(root_done.sem, 1)
                if use == "mix.norm":
                    act.activation(r_col[:, 0:4], ps[:, bank(US[use]), 400:404], ACT.Sqrt, bias=eps[:, 0:1])
                    act.activation(r_col[0:64, 4:5], ps[0:64, bank(US[use]), 404:405], ACT.Sqrt,
                                   bias=eps[0:64, 0:1]) \
                       .then_inc(root_done.sem, 1)

            def xg_split(layer, t, set_no, gain):
                act.activation(xg_hi[:, t, :], h[:, t, :], ACT.Copy, scale=par[:, gain + t:gain + t + 1]) \
                   .then_inc(xhi_ready.sem, 1)

            act.wait_ge(x_in.sem, 32)
            for t in range(KD):
                xg_split(0, t, 0, PAR["next"])
            for n in range(AHEAD):
                split_hi(0, n)
            act.wait_ge(lb_step.sem, 3)
            act.activation(lbt[:, 1:3, :], lbt[:, 1:3, :], ACT.Exp).then_inc(lb_exp.sem, 1)

            def ffn(L, f):
                for g, pairs in enumerate(FF_GROUPS):
                    c0, u0 = CH[f"{f}.{g}.up0"], US[f"{f}.{g}.up0"]
                    j0 = hid_before(f, g)

                    def two_pairs(i, c, u, tile, first):
                        for pr in range(2):
                            step(L, c + 2 * pr, i)
                            if first and pr == 0:
                                step(L, c + 1, i)
                                root(L, f"{f}.norm", 1.0, r[:, :], 0)
                            ug = u + 2 * pr + (1 if first and pr else 0)
                            act.wait_ge(drained.sem, drained.at(L, ug + 1, i * 4))
                            act.activation(gate[:, pr, :], gate[:, pr, :], ACT.Silu).then_inc(silu_done.sem, 1)
                            if not (first and pr == 0):
                                step(L, c + 2 * pr + 1, i)
                            act.wait_ge(prod_done.sem, prod_done.at(L, j0 + tile + pr + 1, i * 2))
                            act.activation(hid_hi[:, tile + pr + i * 2, :], val[:, pr, :], ACT.Copy) \
                               .then_inc(hidhi_ready.sem, 1)

                    if g == 0:
                        two_pairs(0, c0, u0, 0, True)
                        with act.Fori(0, pairs // 2 - 1) as i:
                            two_pairs(i, c0 + 4, u0 + 5, 2, False)
                    else:
                        with act.Fori(0, pairs // 2) as i:
                            two_pairs(i, c0, u0, 0, False)
                    d0, v0 = CH[f"{f}.{g}.down0"], US[f"{f}.{g}.down0"]
                    if g < len(FF_GROUPS) - 1:
                        with act.Fori(0, KD // 4) as i:
                            for q in range(4):
                                step(L, d0 + q, i)
                        continue
                    for m in range(KD):
                        step(L, d0 + m)
                        act.wait_ge(drained.sem, drained.at(L, v0 + m + 1))
                        if f == "ffn1" and m == 0:
                            act.wait_ge(layer_in.sem, layer_in.at(L, layer_in.per))
                        xg_split(L, m, 0, PAR["mix"] if f == "ffn1" else PAR["ple"])

            def mixer_inputs(L):
                for name in W_IN:
                    step(L, CH[name])
                    if name == "f1":
                        root(L, "mix.norm", 1.0, r[:, :], 0)
                    if name == "g0":
                        act.wait_ge(drained.sem, drained.at(L, US["q1"] + 1))
                        act.activation(hq[:, :, :], hq[:, :, :], ACT.Silu).then_inc(silu_in.sem, 1)
                    if name == "i0":
                        act.wait_ge(drained.sem, drained.at(L, US["g1"] + 1))
                        act.activation(hg[:, :, :], hg[:, :, :], ACT.Silu).then_inc(silu_in.sem, 1)
                    if name == "swk":
                        root(L, "ckv.norm", D_MODEL / 128, tmp[:, 5, :], 0)
                    if name == "swv":
                        root(L, "cq.norm", D_MODEL / 256, tmp[:, 1, :], 0)

            def hgrn(L):
                act.wait_ge(drained.sem, drained.at(L, US["f1"] + 1))
                act.activation(fx[:, :, :], fx[:, :, :], ACT.Exp, scale=-1.0).then_inc(f_exp.sem, 1)
                act.wait_ge(f_step.sem, f_step.at(L, 7))
                act.activation(fx[:, :, :], fx[:, :, :], ACT.Ln).then_inc(f_ln.sem, 1)
                act.wait_ge(G_ready.sem, G_ready.at(L, 10))
                act.activation(tmp[:, 0:2, :], G[:, :, :], ACT.Exp).then_inc(eG_ready.sem, 1)
                act.wait_ge(kd_diff.sem, kd_diff.at(L, 3))
                act.activation(tmp[:, 2:4, :], tmp[:, 2:4, :], ACT.Exp).then_inc(kd_exp.sem, 1)
                act.wait_ge(kd_turned.sem, kd_turned.at(L, 1))
                for j in range(2):
                    act.activation(kdT[:, j, 0:4, :], ps[:, 2 * j, :].rearrange("p (b k) -> p b k", b=4),
                                   ACT.Copy).then_inc(kdT_ready.sem, 1)
                    act.activation(kdT[0:64, j, 4, :], ps[0:64, 2 * j + 1, 0:P], ACT.Copy) \
                       .then_inc(kdT_ready.sem, 1)
                for n in range(2 * LEVELS):
                    j, lv = divmod(n, LEVELS)
                    if lv:
                        width = PROMPT if lv == LEVELS - 1 else TOK
                        act.wait_ge(lv_diff.sem, lv_diff.at(L, 2 * (n - j)))
                        act.activation(tmp[:, n % 2, 0:width], tmp[:, n % 2, 0:width], ACT.Exp) \
                           .then_inc(lv_exp.sem, 1)
                    if n == LEVELS + 2:
                        head_out(L, 0)
                head_out(L, 1)
                act.wait_ge(O_out.sem, O_out.at(L, 4))
                act.activation(tmp[:, 0:2, :], hk[:, :, :], ACT.Square).then_inc(O_sq.sem, 1)
                act.wait_ge(O_ms.sem, O_ms.at(L, 1))
                for j in range(2):
                    act.activation(halves(tmp[:, 2 + j, :]), ps[:, 2 * j:2 * j + 2, 0:HALF], ACT.Sqrt,
                                   bias=eps[:, 0:1]).then_inc(O_root.sem, 1)
                act.wait_ge(O_norm.sem, O_norm.at(L, 3))
                act.activation(hid_hi[:, 6:8, :], tmp[:, 4:6, :], ACT.Copy).then_inc(O_hi.sem, 1)

            def head_out(L, j):
                act.wait_ge(O_made.sem, O_made.at(L, j + 1))
                act.wait_ge(lv_qk.sem, lv_qk.at(L, 14 * (j + 1)))
                act.activation(hk[:, j, 0:PROMPT], ps[:, 6, :], ACT.Copy, scale=0.125).then_inc(O_out.sem, 1)
                act.activation(hk[:, j, PROMPT:], ps[:, 7, 0:SAMPLE], ACT.Copy, scale=0.125) \
                   .then_inc(O_out.sem, 1)

            def attention(L):
                x, un = 0, 0
                for kind in ("swa", "mla"):
                    for pr in range(3):
                        if kind == "mla":
                            act.wait_ge(s_made[x % 2].sem, s_made[x % 2].at(L, x // 2 + 1))
                            act.wait_ge(pv_done.sem, pv_done.at(L, un))
                            flat = ps[:, 2 * (x % 2):2 * (x % 2) + 2, :].rearrange("p a n -> p (a n)")
                            act.activation(kT[0][0:64, 0:1024], flat[0:64, :], ACT.Copy)
                            act.activation(kT[1][0:64, 0:1024], flat[64:P, :], ACT.Copy) \
                               .then_inc(s_free[x % 2].sem, 1)
                            x += 1
                            act.wait_ge(s_made[x % 2].sem, s_made[x % 2].at(L, x // 2 + 1))
                            for a in range(2):
                                act.activation(kT[a][0:64, 1024:], ps[64 * a:64 * a + 64, 2 * (x % 2), 0:64],
                                               ACT.Copy)
                            act.activation(mv[0:64, 8, :], ps[0:64, 2 * (x % 2) + 1, 0:P], ACT.Copy) \
                               .then_inc(s_free[x % 2].sem, 1)
                            x += 1
                            act.wait_ge(s_made[x % 2].sem, s_made[x % 2].at(L, x // 2 + 1))
                            act.activation(mv[:, 0:8, :].rearrange("p (a t) v -> p a (t v)", a=2),
                                           ps[:, 2 * (x % 2):2 * (x % 2) + 2, :], ACT.Copy) \
                               .then_inc(s_free[x % 2].sem, 1)
                            x += 4

                        def softmax_exp(v):
                            b = v % 2
                            nq, nk = UNIT_Q[v % 5], unit_keys(kind, v % 5)
                            act.wait_ge(bound_done.sem, bound_done.at(L, un + v + 1))
                            if un + v >= 2:
                                act.wait_ge(turned.sem, turned.at(L, un + v - 1))
                            src = score[0:nq, b, 0:nk] if kind == "swa" else s_flat(x0 + v)[0:nq, 0:nk]
                            act.activation(prob[0:nq, b, 0:nk], src, ACT.Exp, bias=stat[0:nq, b, 1:2],
                                           scale=SWA_SCALE if kind == "swa" else MLA_SCALE,
                                           accum_out=stat[0:nq, b, 2:3]).then_inc(exp_done.sem, 1)
                            if kind == "swa":
                                hd = pr + 3 * (v // 5)
                                act.activation(stat[0:nq, b, 3:4], par[0:nq, PAR["sink"] + hd:PAR["sink"] + hd + 1],
                                               ACT.Exp, bias=stat[0:nq, b, 1:2]).then_inc(sink_done.sem, 1)

                        def copy_t(v):
                            tiles = unit_tiles(kind, v % 5)
                            nq = UNIT_Q[v % 5]
                            act.wait_ge(turned.sem, turned.at(L, un + v + 1))
                            if un + v >= 2:
                                act.wait_ge(pv_done.sem, pv_done.at(L, un + v - 1))
                            full = len(tiles) - (1 if v % 5 == 4 else 0)
                            if full < len(tiles):
                                act.activation(probT[0:64, v % 2, full * nq:(full + 1) * nq],
                                               ps[0:64, 4 + v % 2, full * nq:(full + 1) * nq], ACT.Copy)
                            act.activation(probT[:, v % 2, 0:full * nq], ps[:, 4 + v % 2, 0:full * nq], ACT.Copy) \
                               .then_inc(probT_ready.sem, 1)

                        x0 = x
                        softmax_exp(0)
                        softmax_exp(1)
                        copy_t(0)
                        for v in range(10):
                            if v + 2 < 10:
                                softmax_exp(v + 2)
                            if v + 1 < 10:
                                copy_t(v + 1)
                        tile = pr + (3 if kind == "swa" else 0)
                        act.wait_ge(pv_done.sem, pv_done.at(L, un + 10))
                        act.activation(hid_hi[:, tile, 0:PROMPT], ps[:, 6, :], ACT.Copy).then_inc(att_hi.sem, 1)
                        act.activation(hid_hi[:, tile, PROMPT:], ps[:, 7, 0:SAMPLE], ACT.Copy) \
                           .then_inc(att_hi.sem, 1)
                        x += 10
                        un += 10

            def s_flat(x):
                return ps[:, 2 * (x % 2):2 * (x % 2) + 2, :].rearrange("p a n -> p (a n)")

            with act.Fori(0, DEPTH) as L:
                ffn(L, "ffn1")
                mixer_inputs(L)
                hgrn(L)
                attention(L)
                for m in range(KD):
                    step(L, CH[f"out{m}"])
                    act.wait_ge(drained.sem, drained.at(L, US[f"out{m}"] + 1))
                    xg_split(L, m, 0, PAR["ffn2"])
                act.activation(p_hi[:, :, :], p_raw[:, :, :], ACT.Copy).then_inc(p_split.sem, 1)
                ffn(L, "ffn2")
                for half in range(2):
                    step(L, CH[f"proj{half}"])
                    for m in range(4 * half, 4 * half + 4):
                        step(L, CH[f"gate{m}"])
                        if m == 0:
                            root(L, "ple.norm", 1.0, r[:, :], 0)
                        act.wait_ge(drained.sem, drained.at(L, US[f"gate{m}"] + 1))
                        act.activation(gate[:, m % 2, :], gate[:, m % 2, :], ACT.Sigmoid) \
                           .then_inc(sig_done.sem, 1)
                for t in range(KD):
                    act.wait_ge(h_emb.sem, h_emb.at(L, t + 1))
                    xg_split(L, t, 0, PAR["next"])
            act.wait_ge(made.sem, DEPTH * N_US + made.seed + 1)
            act.activation(halves(r[:, :]), slot(0), ACT.Sqrt, bias=eps[:, 0:1]).then_inc(root_done.sem, 1)

        @block.vector
        def _(dve):
            dve.memset(eps[:, :], EPS).then_inc(drained.sem, 4)
            dve.memset(no_sink[:, :], 0.0).then_inc(wlo_ready.sem, RAW_SLOTS)
            dve.memset(r_col[:, :], 1.0)
            dve.memset(lb[:, :], 0.0).then_inc(set_up.sem, 1)

            def split_lo(layer, n, more=0):
                s = n % W_SLOTS
                dve.wait_ge(whi_ready.sem, whi_ready.at(layer, n + 1, more * 4))
                dve.tensor_tensor(w_lo[:, s, :], w_raw[:, n % RAW_SLOTS, :], w_hi[:, s, :].bitcast(F32),
                                  ALU.subtract).then_inc(wlo_ready.sem, 1)

            def step(layer, n, more=0):
                split_lo(layer, n + AHEAD, more) if n + AHEAD < N_CH else split_lo(layer + 1, n + AHEAD - N_CH, more)

            def inverse(layer, use, roots, out, early=None):
                dve.wait_ge(root_done.sem, root_done.at(layer, roots))
                if use == "mix.norm":
                    dve.reciprocal(r_col[:, :], r_col[:, :])
                if early is None:
                    dve.reciprocal(out, out).then_inc(drained.sem, 1)
                    dve.wait_ge(drained.sem, drained.at(layer, US[use] + 1))
                else:
                    dve.reciprocal(out, out).then_inc(inverted.sem, 1)
                    dve.wait_ge(inverted.sem, inverted.at(layer, early))

            def scaled(layer, u, out, more=0):
                dve.wait_ge(made.sem, made.at(layer, u + 1, more * 4))
                return dve.tensor_tensor(out, slot(u), halves(r[:, :]), ALU.mult)

            def xg_rest(layer, t, count, gain):
                dve.wait_ge(xhi_ready.sem, count)
                dve.scalar_tensor_tensor(xg_lo[:, t, :], h[:, t, :], par[:, gain + t:gain + t + 1],
                                         xg_hi[:, t, :].bitcast(F32), ALU.mult, ALU.subtract) \
                   .then_inc(xg_ready.sem, 1)

            dve.wait_ge(x_in.sem, 32)
            for t in range(KD):
                xg_rest(0, t, t + 1, PAR["next"])
            for n in range(AHEAD):
                split_lo(0, n)
            dve.wait_ge(const_in.sem, 16 * 9)
            dve.tensor_copy(mask[:, :, :], mask_f[:, :, :])
            dve.tensor_tensor(lbt[:, 0, :], lbl[:, 0, :], lbl[:, 1, :], ALU.max).then_inc(lb_step.sem, 1)
            dve.wait_ge(lb_step.sem, 1)
            dve.tensor_tensor(lbt[:, 1, :], lbl[:, 0, :], lbt[:, 0, :], ALU.subtract).then_inc(lb_step.sem, 1)
            dve.tensor_tensor(lbt[:, 2, :], lbl[:, 1, :], lbt[:, 0, :], ALU.subtract).then_inc(lb_step.sem, 1)
            dve.wait_ge(lb_exp.sem, 1)
            dve.tensor_tensor(lbt[:, 3, :], lbt[:, 1, :], lbt[:, 2, :], ALU.add).then_inc(lb_step.sem, 1)
            dve.wait_ge(lb_step.sem, 4)
            dve.reciprocal(lbt[:, 3, :], lbt[:, 3, :]).then_inc(lb_step.sem, 1)
            dve.wait_ge(lb_step.sem, 5)
            dve.tensor_tensor(lbt[:, 1, :], lbt[:, 1, :], lbt[:, 3, :], ALU.mult).then_inc(lb_step.sem, 1)
            dve.tensor_tensor(lbt[:, 2, :], lbt[:, 2, :], lbt[:, 3, :], ALU.mult).then_inc(lb_step.sem, 1)
            dve.wait_ge(lb_step.sem, 7)
            dve.tensor_tensor(lbt[:, 2, :], lbt[:, 2, :], lbt[:, 1, :], ALU.add).then_inc(lb_step.sem, 1)
            dve.wait_ge(lb_step.sem, 8)
            dve.tensor_tensor(lb_next[:, :], lbt[:, 2, :], lbt[:, 1, :], ALU.subtract).then_inc(lb_step.sem, 1)
            dve.wait_ge(lb_step.sem, 9)

            def ffn(L, f):
                roots = 1 if f == "ffn1" else 6
                for g, pairs in enumerate(FF_GROUPS):
                    c0, u0 = CH[f"{f}.{g}.up0"], US[f"{f}.{g}.up0"]
                    j0 = hid_before(f, g)

                    def two_pairs(i, c, u, tile, first):
                        for pr in range(2):
                            step(L, c + 2 * pr, i)
                            if first and pr == 0:
                                step(L, c + 1, i)
                                inverse(L, f"{f}.norm", roots, r[:, :], 1 if f == "ffn1" else 3)
                            ug = u + 2 * pr + (1 if first and pr else 0)
                            scaled(L, ug, halves(gate[:, pr, :]), i).then_inc(drained.sem, 1)
                            if not (first and pr == 0):
                                step(L, c + 2 * pr + 1, i)
                            scaled(L, ug + 1, halves(val[:, pr, :]), i) \
                                .then_inc(drained.sem, 2 if first and pr == 0 else 1)
                            j = j0 + tile + pr
                            dve.wait_ge(drained.sem, drained.at(L, ug + 2, i * 4))
                            dve.wait_ge(silu_done.sem, silu_done.at(L, j + 1, i * 2))
                            dve.tensor_tensor(val[:, pr, :], gate[:, pr, :], val[:, pr, :], ALU.mult) \
                               .then_inc(prod_done.sem, 1)
                            dve.wait_ge(hidhi_ready.sem, hidhi_ready.at(L, j + 1, i * 2))
                            dve.tensor_tensor(hid_lo[:, tile + pr + i * 2, :], val[:, pr, :],
                                              hid_hi[:, tile + pr + i * 2, :].bitcast(F32), ALU.subtract) \
                               .then_inc(hid_ready.sem, 1)

                    if g == 0:
                        two_pairs(0, c0, u0, 0, True)
                        with dve.Fori(0, pairs // 2 - 1) as i:
                            two_pairs(i, c0 + 4, u0 + 5, 2, False)
                    else:
                        with dve.Fori(0, pairs // 2) as i:
                            two_pairs(i, c0, u0, 0, False)
                    d0, v0 = CH[f"{f}.{g}.down0"], US[f"{f}.{g}.down0"]

                    def down(m, q, i):
                        dve.wait_ge(made.sem, made.at(L, v0 + q + 1, i * 4))
                        dve.scalar_tensor_tensor(halves(h[:, m, :]), slot(v0 + q), 0.5, halves(h[:, m, :]),
                                                 ALU.mult, ALU.add).then_inc(drained.sem, 1)

                    if g < len(FF_GROUPS) - 1:
                        with dve.Fori(0, KD // 4) as i:
                            for q in range(4):
                                step(L, d0 + q, i)
                                down(q + i * 4, q, i)
                        continue
                    gain, before = (PAR["mix"], 0) if f == "ffn1" else (PAR["ple"], 16)
                    for m in range(KD):
                        step(L, d0 + m)
                        down(m, m, 0)
                        if m:
                            xg_rest(L, m - 1, xhi_ready.at(L, before + m), gain)
                    xg_rest(L, KD - 1, xhi_ready.at(L, before + KD), gain)

            def mixer_inputs(L):
                for name in W_IN:
                    step(L, CH[name])
                    if name == "f0" or name == "spare":
                        continue
                    if name == "f1":
                        inverse(L, "mix.norm", 3, r[:, :], 2)
                        for j in range(2):
                            scaled(L, US[f"f{j}"], halves(fx[:, j, :])).then_inc(drained.sem, 1 + j)
                        continue
                    u = US[name]
                    if name[0] in "qg":
                        dst = (hq if name[0] == "q" else hg)[:, int(name[1]), :]
                        scaled(L, u, halves(dst)).then_inc(drained.sem, 1)
                    elif name in ("i0", "i1", "swv"):
                        dve.wait_ge(made.sem, made.at(L, u + 1))
                        for b in range(5):
                            rows = P if b < 4 else 64
                            if name == "swv":
                                dst = swv[0:rows, b if b < 4 else 5, :]
                            else:
                                dst = V[0:rows, b, 128 * int(name[1]):128 * int(name[1]) + 128]
                            src = ps[0:rows, bank(u) + b // 4, 128 * (b % 4):128 * (b % 4) + 128]
                            ins = dve.tensor_scalar(dst, src, r_col[0:rows, b:b + 1], None, ALU.mult)
                        ins.then_inc(drained.sem, 1)
                    elif name == "ckv":
                        scaled(L, u, halves(tmp[:, 0, :])).then_inc(drained.sem, 1)
                    elif name == "kr":
                        scaled(L, u, halves(tmp[:, 2, :])).then_inc(drained.sem, 1)
                        dve.wait_ge(drained.sem, drained.at(L, u + 1))
                        dve.tensor_tensor(tmp[:, 2, :], tmp[:, 2, :], cs[:, :], ALU.mult).then_inc(c_raw.sem, 1)
                    elif name in ("cq0", "cq1"):
                        scaled(L, u, halves(cq[:, int(name[2]), :])).then_inc(drained.sem, 1)
                    elif name == "swk":
                        inverse(L, "ckv.norm", 4, tmp[:, 5, :])
                        for lo, hi, to in ((0, PROMPT, 0), (PROMPT, TOK, PROMPT + PAST)):
                            dve.scalar_tensor_tensor(ckv[:, to:to + hi - lo], tmp[:, 0, lo:hi],
                                                     par[:, PAR["kv_norm"]:PAR["kv_norm"] + 1],
                                                     tmp[:, 5, lo:hi], ALU.mult, ALU.mult).then_inc(c_norm.sem, 1)
                        dve.wait_ge(made.sem, made.at(L, u + 1))
                        flat = ps[:, bank(u):bank(u) + 2, 0:HALF]
                        dve.tensor_tensor(swk[:, 0:HALF], ps[:, bank(u), 0:HALF], r[:, 0:HALF], ALU.mult) \
                           .then_inc(c_norm.sem, 1)
                        dve.tensor_tensor(swk[:, HALF:PROMPT], ps[:, bank(u) + 1, 0:PROMPT - HALF],
                                          r[:, HALF:PROMPT], ALU.mult).then_inc(c_norm.sem, 1)
                        dve.tensor_tensor(swk[:, PROMPT + 128:], ps[:, bank(u) + 1, PROMPT - HALF:HALF],
                                          r[:, PROMPT:], ALU.mult).then_inc(drained.sem, 1)
                        dve.wait_ge(made.sem, made.at(L, US["kr.sum"] + 1))
                        dve.tensor_copy(halves(krs[64:96, :]),
                                        ps[64:96, bank(US["kr.sum"]):bank(US["kr.sum"]) + 2, 0:HALF]) \
                           .then_inc(drained.sem, 1)
                        inverse(L, "cq.norm", 5, tmp[:, 1, :])
                        for j in range(2):
                            dve.scalar_tensor_tensor(cq[:, j, :], cq[:, j, :],
                                                     par[:, PAR["q_norm"] + j:PAR["q_norm"] + j + 1],
                                                     tmp[:, 1, :], ALU.mult, ALU.mult).then_inc(c_norm.sem, 1)
                    else:
                        scaled(L, u, halves(swq[:, int(name[3]), :])).then_inc(drained.sem, 1)
                dve.tensor_scalar(no_sink[:, :], par[:, PAR["sink"]:PAR["sink"] + 6], -1.0, None, ALU.mult) \
                   .then_inc(c_norm.sem, 1)

            def hgrn(L):
                dve.wait_ge(f_exp.sem, f_exp.at(L, 1))
                dve.tensor_scalar(one_minus_lb[:, :], lb[:, :], -1.0, 1.0, ALU.mult, ALU.add) \
                   .then_inc(f_step.sem, 1)
                dve.tensor_scalar(fx[:, :, :], fx[:, :, :], 1.0, None, ALU.add).then_inc(f_step.sem, 1)
                dve.wait_ge(f_step.sem, f_step.at(L, 2))
                dve.reciprocal(fx[:, :, :], fx[:, :, :]).then_inc(f_step.sem, 1)
                dve.wait_ge(f_step.sem, f_step.at(L, 3))
                for j in range(2):
                    dve.tensor_scalar(fx[:, j, :], fx[:, j, :], one_minus_lb[:, j:j + 1], lb[:, j:j + 1],
                                      ALU.mult, ALU.add).then_inc(f_step.sem, 1)
                dve.wait_ge(f_step.sem, f_step.at(L, 5))
                dve.tensor_scalar(hk[:, :, :], fx[:, :, :], -1.0, 1.0, ALU.mult, ALU.add).then_inc(f_step.sem, 1)
                dve.tensor_scalar(fx[:, :, :], fx[:, :, :], TINY, None, ALU.max).then_inc(f_step.sem, 1)
                dve.tensor_copy(lb[:, :], lb_next[:, :]).then_inc(f_step.sem, 1)
                dve.wait_ge(f_ln.sem, f_ln.at(L, 1))
                for j in range(2):
                    for t0, tn in BLOCKS:
                        dve.tensor_tensor_scan(G[:, j, t0:t0 + tn], fx[:, j, t0:t0 + tn], fx[:, j, t0:t0 + tn],
                                               0.0, ALU.add, ALU.bypass).then_inc(G_ready.sem, 1)
                dve.wait_ge(G_ready.sem, G_ready.at(L, 10))
                for j in range(2):
                    g4 = G[:, j, 0:PROMPT].rearrange("p (b t) -> p b t", b=4)
                    dve.tensor_tensor(tmp[:, 2 + j, 0:PROMPT].rearrange("p (b t) -> p b t", b=4),
                                      g4[:, :, P - 1:P].to_broadcast([P, 4, P]), g4, ALU.subtract) \
                       .then_inc(kd_diff.sem, 1)
                dve.tensor_tensor(tmp[:, 2:4, PROMPT:], G[:, :, TOK - 1:TOK].to_broadcast([P, 2, SAMPLE]),
                                  G[:, :, PROMPT:], ALU.subtract).then_inc(kd_diff.sem, 1)
                dve.wait_ge(eG_ready.sem, eG_ready.at(L, 1))
                dve.wait_ge(silu_in.sem, silu_in.at(L, 2))
                dve.tensor_tensor(qG[:, :, :], hq[:, :, :], tmp[:, 0:2, :], ALU.mult).then_inc(qG_ready.sem, 1)
                dve.tensor_copy(e_end[:, :, 0:4], tmp[:, 0:2, P - 1:PROMPT:P]).then_inc(qG_ready.sem, 1)
                dve.tensor_copy(e_end[:, :, 4:5], tmp[:, 0:2, TOK - 1:TOK]).then_inc(qG_ready.sem, 1)
                dve.wait_ge(kd_exp.sem, kd_exp.at(L, 1))
                dve.tensor_tensor(tmp[:, 4:6, :], hk[:, :, :], tmp[:, 2:4, :], ALU.mult).then_inc(kd_ready.sem, 1)
                dve.wait_ge(qG_ready.sem, qG_ready.at(L, 3))
                dve.wait_ge(dS_made.sem, dS_made.at(L, 1))
                for b in range(4):
                    for j in range(2):
                        d = ps[:, 4 + j, 64 * b:64 * b + 64]
                        if b == 0:
                            dve.tensor_copy(S[:, j, 1, :], d).then_inc(S_ready.sem, 1)
                            continue
                        dve.wait_ge(S_ready.sem, S_ready.at(L, 2 * b + j - 1))
                        dve.scalar_tensor_tensor(S[:, j, b + 1, :], S[:, j, b, :], e_end[:, j, b:b + 1], d,
                                                 ALU.mult, ALU.add).then_inc(S_ready.sem, 1)
                for j in range(2):
                    dve.scalar_tensor_tensor(S[:, j, 6, :], S[:, j, 5, :], e_end[:, j, 4:5],
                                             ps[:, 4 + j, 256:320], ALU.mult, ALU.add).then_inc(S_ready.sem, 1)

                def diff(n):
                    j, lv = divmod(n, LEVELS)
                    if lv == 0:
                        return
                    m = 1 << lv
                    width = PROMPT if m == P else TOK
                    g = G[:, j, 0:width].rearrange("p (s t) -> p s t", t=m)
                    e = tmp[:, n % 2, 0:width].rearrange("p (s t) -> p s t", t=m)
                    mid = g[:, :, m // 2 - 1:m // 2].to_broadcast([P, width // m, m // 2])
                    before = n - 2 - (n - 2) // LEVELS
                    if before > 0:
                        dve.wait_ge(lv_qk.sem, lv_qk.at(L, 2 * before))
                    dve.tensor_tensor(e[:, :, 0:m // 2], mid, g[:, :, 0:m // 2], ALU.subtract) \
                       .then_inc(lv_diff.sem, 1)
                    dve.tensor_tensor(e[:, :, m // 2:], g[:, :, m // 2:], mid, ALU.subtract) \
                       .then_inc(lv_diff.sem, 1)

                def products(n):
                    j, lv = divmod(n, LEVELS)
                    if lv == 0:
                        return
                    width = PROMPT if lv == LEVELS - 1 else TOK
                    dve.wait_ge(lv_exp.sem, lv_exp.at(L, n - j))
                    e = tmp[:, n % 2, 0:width]
                    dve.tensor_tensor(tmp[:, 2 + n % 2, 0:width], hq[:, j, 0:width], e, ALU.mult) \
                       .then_inc(lv_qk.sem, 1)
                    dve.tensor_tensor(tmp[:, 4 + n % 2, 0:width], hk[:, j, 0:width], e, ALU.mult) \
                       .then_inc(lv_qk.sem, 1)

                def take(n):
                    j, lv = divmod(n, LEVELS)
                    big = ps[:, 3 * (n % 2):3 * (n % 2) + 2, :].rearrange("p a (b t) -> p (a b) t", b=4)
                    small = ps[0:64, 3 * (n % 2) + 2, 0:128].rearrange("p (a t) -> p a t", a=2)
                    dve.wait_ge(A_made.sem, A_made.at(L, n + 1))
                    a8 = A[:, :, :, :].rearrange("p a b t -> p (a b) t")
                    if lv == 0:
                        if j:
                            dve.wait_ge(O_made.sem, O_made.at(L, 1))
                        dve.tensor_tensor(a8, big, ident[:, :].unsqueeze(1).to_broadcast([P, 8, P]), ALU.mult) \
                           .then_inc(A_taken.sem, 1)
                        dve.tensor_tensor(a_tail[:, :, :], small,
                                          ident[0:64, 0:64].unsqueeze(1).to_broadcast([64, 2, 64]), ALU.mult) \
                           .then_inc(A_taken.sem, 1)
                        return
                    dve.wait_ge(A_taken.sem, A_taken.at(L, 2 * n))
                    by_itself(dve)
                    mk = mask[:, lv - 1, :]
                    ins = dve.copy_predicated(a8, mk.unsqueeze(1).to_broadcast([P, 8, P]), big)
                    if lv == LEVELS - 1:
                        ins.then_inc(A_taken.sem, 2)
                        return
                    ins.then_inc(A_taken.sem, 1)
                    dve.copy_predicated(a_tail[:, :, :],
                                        mask[0:64, lv - 1, 0:64].unsqueeze(1).to_broadcast([64, 2, 64]), small) \
                       .then_inc(A_taken.sem, 1)

                n_steps = 2 * LEVELS
                for n in range(n_steps + 1):
                    if n + 1 < n_steps:
                        diff(n + 1)
                    if n < n_steps:
                        products(n)
                    if n:
                        take(n - 1)
                dve.wait_ge(O_root.sem, O_root.at(L, 2))
                dve.reciprocal(tmp[:, 2:4, :], tmp[:, 2:4, :]).then_inc(O_norm.sem, 1)
                dve.wait_ge(O_norm.sem, O_norm.at(L, 1))
                flat = lambda t: t.rearrange("p a n -> p (a n)")
                dve.scalar_tensor_tensor(flat(tmp[:, 4:6, :]), flat(hk[:, :, :]),
                                         par[:, PAR["hg_out"]:PAR["hg_out"] + 1], flat(tmp[:, 2:4, :]),
                                         ALU.mult, ALU.mult).then_inc(O_norm.sem, 1)
                dve.wait_ge(O_norm.sem, O_norm.at(L, 2))
                dve.tensor_tensor(tmp[:, 4:6, :], tmp[:, 4:6, :], hg[:, :, :], ALU.mult).then_inc(O_norm.sem, 1)
                dve.wait_ge(O_hi.sem, O_hi.at(L, 1))
                dve.tensor_tensor(hid_lo[:, 6:8, :], tmp[:, 4:6, :], hid_hi[:, 6:8, :].bitcast(F32),
                                  ALU.subtract).then_inc(O_lo.sem, 1)

            def attention(L):
                x, un, swa_n = 0, 0, 0
                for kind in ("swa", "mla"):
                    for pr in range(3):
                        if kind == "mla":
                            x += 3
                            dve.wait_ge(s_made[x % 2].sem, s_made[x % 2].at(L, x // 2 + 1))
                            dve.tensor_tensor(halves(tq[:, :]), ps[:, 2 * (x % 2):2 * (x % 2) + 2, 0:HALF],
                                              halves(cs[:, :]), ALU.mult).then_inc(s_free[x % 2].sem, 1)
                            x += 1
                            for a in range(2):
                                dve.wait_ge(s_made[x % 2].sem, s_made[x % 2].at(L, x // 2 + 1))
                                dve.tensor_copy(halves(qT[a][0:96, :]),
                                                ps[0:96, 2 * (x % 2):2 * (x % 2) + 2, 0:HALF]) \
                                   .then_inc(s_free[x % 2].sem, 1)
                                x += 1

                        x0 = x

                        def bound(v):
                            xs, b = x0 + v, v % 2
                            nq, nk = UNIT_Q[v % 5], unit_keys(kind, v % 5)
                            flat = ps[:, 2 * (xs % 2):2 * (xs % 2) + 2, :].rearrange("p a n -> p (a n)")
                            src = flat[0:nq, 0:nk]
                            dve.wait_ge(s_made[xs % 2].sem, s_made[xs % 2].at(L, xs // 2 + 1))
                            if v >= 2:
                                dve.wait_ge(exp_done.sem, exp_done.at(L, un + v - 1))
                                if kind == "swa":
                                    dve.wait_ge(sink_done.sem, sink_done.at(L, swa_n + v - 1))
                            if kind == "swa":
                                hd = pr + 3 * (v // 5)
                                slope = 2.0 ** (-8.0 * (hd + 1) / 6)
                                k0 = 128 if v % 5 == 0 else 0
                                dve.scalar_tensor_tensor(score[0:nq, b, 0:nk], dist[0:nq, k0:k0 + nk],
                                                         -slope / SWA_SCALE, src, ALU.mult, ALU.add) \
                                   .then_inc(scored.sem, 1)
                                dve.wait_ge(scored.sem, scored.at(L, un + v + 1))
                                dve.reduce_max(stat[0:nq, b, 0:1], score[0:nq, b, 0:nk], AX.X) \
                                   .then_inc(s_free[xs % 2].sem, 1)
                                dve.wait_ge(s_free[xs % 2].sem, s_free[xs % 2].at(L, xs // 2 + 1))
                                dve.tensor_scalar(stat[0:nq, b, 1:2], stat[0:nq, b, 0:1], -SWA_SCALE,
                                                  no_sink[0:nq, hd:hd + 1], ALU.mult, ALU.min) \
                                   .then_inc(bound_done.sem, 1)
                                return
                            dve.reduce_max(stat[0:nq, b, 0:1], src, AX.X).then_inc(scored.sem, 1)
                            dve.wait_ge(scored.sem, scored.at(L, un + v + 1))
                            dve.tensor_scalar(stat[0:nq, b, 1:2], stat[0:nq, b, 0:1], -MLA_SCALE, None,
                                              ALU.mult).then_inc(bound_done.sem, 1)

                        def normalize(v):
                            b = v % 2
                            nq, nk = UNIT_Q[v % 5], unit_keys(kind, v % 5)
                            dve.wait_ge(exp_done.sem, exp_done.at(L, un + v + 1))
                            if kind == "mla":
                                dve.reciprocal(stat[0:nq, b, 4:5], stat[0:nq, b, 2:3]) \
                                   .then_inc(s_free[(x0 + v) % 2].sem, 1)
                                dve.wait_ge(s_free[(x0 + v) % 2].sem,
                                            s_free[(x0 + v) % 2].at(L, (x0 + v) // 2 + 1))
                            else:
                                dve.wait_ge(sink_done.sem, sink_done.at(L, swa_n + v + 1))
                                dve.tensor_tensor(stat[0:nq, b, 3:4], stat[0:nq, b, 2:3], stat[0:nq, b, 3:4],
                                                  ALU.add).then_inc(den_done.sem, 1)
                                dve.wait_ge(den_done.sem, den_done.at(L, swa_n + v + 1))
                                dve.reciprocal(stat[0:nq, b, 4:5], stat[0:nq, b, 3:4]) \
                                   .then_inc(recip_done.sem, 1)
                                dve.wait_ge(recip_done.sem, recip_done.at(L, swa_n + v + 1))
                            dve.tensor_scalar(prob[0:nq, b, 0:nk], prob[0:nq, b, 0:nk], stat[0:nq, b, 4:5],
                                              None, ALU.mult).then_inc(prob_ready.sem, 1)

                        bound(0)
                        bound(1)
                        normalize(0)
                        for v in range(10):
                            if v + 2 < 10:
                                bound(v + 2)
                            if v + 1 < 10:
                                normalize(v + 1)
                        tile, at = pr + (3 if kind == "swa" else 0), 2 * (un // 10)
                        dve.wait_ge(att_hi.sem, att_hi.at(L, at + 2))
                        dve.tensor_tensor(hid_lo[:, tile, 0:PROMPT], ps[:, 6, :],
                                          hid_hi[:, tile, 0:PROMPT].bitcast(F32), ALU.subtract) \
                           .then_inc(att_lo.sem, 1)
                        dve.tensor_tensor(hid_lo[:, tile, PROMPT:], ps[:, 7, 0:SAMPLE],
                                          hid_hi[:, tile, PROMPT:].bitcast(F32), ALU.subtract) \
                           .then_inc(att_lo.sem, 1)
                        x += 10
                        un += 10
                        if kind == "swa":
                            swa_n += 10

            with dve.Fori(0, DEPTH) as L:
                ffn(L, "ffn1")
                mixer_inputs(L)
                hgrn(L)
                attention(L)
                for m in range(KD):
                    step(L, CH[f"out{m}"])
                    u = US[f"out{m}"]
                    dve.wait_ge(made.sem, made.at(L, u + 1))
                    dve.tensor_tensor(halves(h[:, m, :]), slot(u), halves(h[:, m, :]), ALU.add) \
                       .then_inc(drained.sem, 1)
                    if m:
                        xg_rest(L, m - 1, xhi_ready.at(L, 8 + m), PAR["ffn2"])
                xg_rest(L, KD - 1, xhi_ready.at(L, 16), PAR["ffn2"])
                dve.wait_ge(p_split.sem, p_split.at(L, 1))
                dve.tensor_tensor(p_lo[:, :, :], p_raw[:, :, :], p_hi[:, :, :].bitcast(F32), ALU.subtract) \
                   .then_inc(p_ready.sem, 1)
                ffn(L, "ffn2")
                for half in range(2):
                    step(L, CH[f"proj{half}"])
                    for m in range(4):
                        u = US[f"proj{half}.{m}"]
                        dve.wait_ge(made.sem, made.at(L, u + 1))
                        dve.tensor_copy(halves(pp[:, m, :]), slot(u)).then_inc(drained.sem, 1)
                    for m in range(4 * half, 4 * half + 4):
                        step(L, CH[f"gate{m}"])
                        u = US[f"gate{m}"]
                        if m == 0:
                            inverse(L, "ple.norm", 7, r[:, :], 4)
                        last = 1 if m == 0 else PAD_US if m == KD - 1 else 0
                        scaled(L, u, halves(gate[:, m % 2, :])).then_inc(drained.sem, 1 + last)
                        dve.wait_ge(sig_done.sem, sig_done.at(L, m + 1))
                        dve.tensor_tensor(val[:, m % 2, :], gate[:, m % 2, :], pp[:, m % 4, :], ALU.mult) \
                           .then_inc(emb_mul.sem, 1)
                        dve.wait_ge(emb_mul.sem, emb_mul.at(L, m + 1))
                        dve.tensor_tensor(h[:, m, :], h[:, m, :], val[:, m % 2, :], ALU.add) \
                           .then_inc(h_emb.sem, 1)
                for t in range(KD):
                    xg_rest(L, t, xhi_ready.at(L, 24 + t + 1), PAR["next"])
            dve.wait_ge(root_done.sem, DEPTH * root_done.per + 1)
            dve.reciprocal(r[:, :], r[:, :]).then_inc(lb_step.sem, 1)
            dve.wait_ge(lb_step.sem, 10)
            for t in range(KD):
                dve.scalar_tensor_tensor(y[:, t, :], h[:, t, :], par[:, PAR["next"] + t:PAR["next"] + t + 1],
                                         r[:, :], ALU.mult, ALU.mult).then_inc(y_done.sem, 1)

        @block.gpsimd
        def _(pool):
            def square(t, sq_count, acc_count):
                if t == 0:
                    pool.tensor_tensor(acc[:, :], h[:, 0, :], h[:, 0, :], ALU.mult).then_inc(acc_done.sem, 1)
                    return
                pool.wait_ge(acc_done.sem, acc_count)
                pool.tensor_tensor(sq[:, :], h[:, t, :], h[:, t, :], ALU.mult).then_inc(sq_done.sem, 1)
                pool.wait_ge(sq_done.sem, sq_count)
                pool.tensor_tensor(acc[:, :], acc[:, :], sq[:, :], ALU.add).then_inc(acc_done.sem, 1)

            def squares(L, set_no, wait, norm):
                for t in range(KD):
                    wait(t)
                    if t == 0:
                        pool.wait_ge(made.sem, made.at(L, US[norm] + 1))
                    square(t, sq_done.at(L, 7 * set_no + t), acc_done.at(L, 8 * set_no + t))

            pool.wait_ge(x_in.sem, 32)
            for t in range(KD):
                square(t, t, t)

            with pool.Fori(0, DEPTH) as L:
                squares(L, 0, lambda t: pool.wait_ge(drained.sem, drained.at(L, US[f"ffn1.2.down{t}"] + 1)),
                        "ffn1.norm")
                pool.wait_ge(drained.sem, drained.at(L, US["ckv"] + 1))
                pool.tensor_tensor(tmp[:, 1, :], tmp[:, 0, :], tmp[:, 0, :], ALU.mult).then_inc(c_sq.sem, 1)
                for j in range(2):
                    pool.wait_ge(drained.sem, drained.at(L, US[f"cq{j}"] + 1))
                    pool.tensor_tensor(tmp[:, 3 + j, :], cq[:, j, :], cq[:, j, :], ALU.mult).then_inc(c_sq.sem, 1)
                pool.wait_ge(drained.sem, drained.at(L, US["swq2"] + 1))
                by_itself(pool)
                for a in range(2):
                    pool.tensor_copy(kT[a][64:96, 0:PROMPT], krs[64:96, 0:PROMPT]).then_inc(k_placed.sem, 1)
                    pool.tensor_copy(kT[a][64:96, PROMPT + PAST:], krs[64:96, PROMPT:]).then_inc(k_placed.sem, 1)
                squares(L, 1, lambda t: pool.wait_ge(drained.sem, drained.at(L, US[f"out{t}"] + 1)), "mix.norm")
                squares(L, 2, lambda t: pool.wait_ge(drained.sem, drained.at(L, US[f"ffn2.2.down{t}"] + 1)),
                        "ffn2.norm")
                squares(L, 3, lambda t: pool.wait_ge(h_emb.sem, h_emb.at(L, t + 1)), "ple.norm")

        @block.tensor
        def _(pe):
            pe.sem_inc(made.sem, made.seed)
            for parity in range(2):
                pe.sem_inc(s_free[parity].sem, 1)

            def ready(layer, n, u, more=0):
                pe.wait_ge(wlo_ready.sem, wlo_ready.at(layer, n + 1, more * 4))
                pe.wait_ge(drained.sem, layer * N_US + (u + 1) + more * 4)

            def dense(n, u, src_hi, src_lo, kts, w_at=lambda k: k * P, wait=None):
                s = n % W_SLOTS
                for k in kts:
                    if wait is not None:
                        wait(k)
                    wh, wl = (w[:, s, w_at(k):w_at(k) + P] for w in (w_hi, w_lo))
                    for i, (w, m) in enumerate(((wh, src_hi), (wh, src_lo), (wl, src_hi))):
                        for c in range(2):
                            ins = pe.matmul(ps[:, bank(u) + c, 0:HALF], w, m[:, k, c * HALF:(c + 1) * HALF],
                                            start=(k == kts[0] and i == 0), stop=(k == kts[-1] and i == 2))
                return ins

            def norm(layer, use, acc_count, columns=False):
                u = US[use]
                pe.wait_ge(drained.sem, layer * N_US + (u + 1))
                pe.wait_ge(acc_done.sem, acc_count)
                if columns:
                    for b, (t0, tn) in enumerate(BLOCKS):
                        pe.matmul(ps[0:tn, bank(u), 400 + b:401 + b], acc[:, t0:t0 + tn], ones[:, 0:1],
                                  start=True, stop=True)
                for c in range(2):
                    ins = pe.matmul(ps[:, bank(u) + c, 0:HALF], ones[:, :], acc[:, c * HALF:(c + 1) * HALF],
                                    start=True, stop=True)
                ins.then_inc(made.sem, 1)

            KT = tuple(range(KD))

            def xg_wait(count):
                return lambda k: pe.wait_ge(xg_ready.sem, count + k)

            def ffn(L, f):
                set_no = 0 if f == "ffn1" else 2
                for g, pairs in enumerate(FF_GROUPS):
                    c0, u0 = CH[f"{f}.{g}.up0"], US[f"{f}.{g}.up0"]

                    def four(i, c, u, first):
                        for q in range(4):
                            uq_ = u + q + (1 if first and q > 1 else 0)
                            ready(L, c + q, uq_, i)
                            wait = xg_wait(L * 32 + (8 * set_no + 1)) if first and q == 0 else None
                            dense(c + q, uq_, xg_hi, xg_lo, KT, wait=wait).then_inc(made.sem, 1)
                            if first and q == 1:
                                norm(L, f"{f}.norm", L * 32 + 8 * (set_no + 1))

                    if g == 0:
                        four(0, c0, u0, True)
                        with pe.Fori(0, pairs // 2 - 1) as i:
                            four(i, c0 + 4, u0 + 5, False)
                    else:
                        with pe.Fori(0, pairs // 2) as i:
                            four(i, c0, u0, False)
                    d0, v0 = CH[f"{f}.{g}.down0"], US[f"{f}.{g}.down0"]
                    j0 = hid_before(f, g)
                    with pe.Fori(0, KD // 4) as i:
                        for q in range(4):
                            ready(L, d0 + q, v0 + q, i)
                            wait = (lambda k: pe.wait_ge(hid_ready.sem, hid_ready.at(L, j0 + k + 1))) \
                                if q == 0 else None
                            dense(d0 + q, v0 + q, hid_hi, hid_lo, tuple(range(pairs)), wait=wait) \
                                .then_inc(made.sem, 1)

            def mixer_inputs(L):
                for name in W_IN:
                    n = CH[name]
                    if name == "spare":
                        pe.wait_ge(wlo_ready.sem, wlo_ready.at(L, n + 1))
                        continue
                    u = US[name]
                    ready(L, n, u)
                    if name in ("i0", "i1", "swv"):
                        s = n % W_SLOTS
                        for b, (t0, tn) in enumerate(BLOCKS):
                            out = ps[0:tn, bank(u) + b // 4, 128 * (b % 4):128 * (b % 4) + 128]
                            for k in KT:
                                for i, (a, w) in enumerate(((xg_hi, w_hi), (xg_hi, w_lo), (xg_lo, w_hi))):
                                    ins = pe.matmul(out, a[:, k, t0:t0 + tn], w[:, s, k * P:(k + 1) * P],
                                                    start=(k == 0 and i == 0), stop=(k == KD - 1 and i == 2))
                        ins.then_inc(made.sem, 1)
                    else:
                        wait = xg_wait(L * 32 + 9) if name == "f0" else None
                        dense(n, u, xg_hi, xg_lo, KT, wait=wait).then_inc(made.sem, 1)
                    if name == "f1":
                        norm(L, "mix.norm", L * 32 + 16, columns=True)
                    if name == "cq1":
                        small_sum(L, "ckv.norm", [tmp[:, 1, :]], ones[:, :], c_sq.at(L, 1))
                    if name == "swk":
                        u = US["kr.sum"]
                        pe.wait_ge(drained.sem, L * N_US + (u + 1))
                        pe.wait_ge(c_raw.sem, c_raw.at(L, 1))
                        for c in range(2):
                            ins = pe.matmul(ps[0:96, bank(u) + c, 0:HALF], comb[0:64, 0, :],
                                            tmp[0:64, 2, c * HALF:(c + 1) * HALF], start=True, stop=True)
                        ins.then_inc(made.sem, 1)
                        small_sum(L, "cq.norm", [tmp[:, 3, :], tmp[:, 4, :]], ones[:, :], c_sq.at(L, 3))

            def small_sum(L, use, srcs, lhs, count):
                u = US[use]
                pe.wait_ge(drained.sem, L * N_US + (u + 1))
                pe.wait_ge(c_sq.sem, count)
                for i, src in enumerate(srcs):
                    for c in range(2):
                        ins = pe.matmul(ps[:, bank(u) + c, 0:HALF], lhs, src[:, c * HALF:(c + 1) * HALF],
                                        start=(i == 0), stop=(i == len(srcs) - 1))
                ins.then_inc(made.sem, 1)

            def hgrn(L):
                pe.wait_ge(drained.sem, drained.at(L, US["swq2"] + 1))
                pe.wait_ge(kd_ready.sem, kd_ready.at(L, 1))
                for j in range(2):
                    for b, (t0, tn) in enumerate(BLOCKS):
                        ins = pe.transpose(ps[0:tn, 2 * j + b // 4, 128 * (b % 4):128 * (b % 4) + 128],
                                           tmp[:, 4 + j, t0:t0 + tn], ident[:, :])
                ins.then_inc(kd_turned.sem, 1)
                pe.wait_ge(kdT_ready.sem, kdT_ready.at(L, 4))
                for j in range(2):
                    for a in range(2):
                        for b, (t0, tn) in enumerate(BLOCKS):
                            ins = pe.matmul(ps[64 * a:64 * a + 64, 4 + j, 64 * b:64 * b + 64],
                                            kdT[0:tn, j, b, 64 * a:64 * a + 64],
                                            V[0:tn, b, 128 * j + 64 * a:128 * j + 64 * a + 64],
                                            start=True, stop=True)
                ins.then_inc(dS_made.sem, 1)
                pe.wait_ge(S_ready.sem, S_ready.at(L, 10))
                for n in range(2 * LEVELS):
                    j, lv = divmod(n, LEVELS)
                    if lv:
                        pe.wait_ge(lv_qk.sem, lv_qk.at(L, 2 * (n - j)))
                        q, k = tmp[:, 2 + n % 2, :], tmp[:, 4 + n % 2, :]
                    else:
                        q, k = hq[:, j, :], hk[:, j, :]
                    if n >= 2:
                        pe.wait_ge(A_taken.sem, A_taken.at(L, 2 * (n - 1)))
                    by_itself(pe)
                    blocks = BLOCKS[:4] if lv == LEVELS - 1 else BLOCKS
                    for a in range(2):
                        rows = slice(64 * a, 64 * a + 64)
                        order = sorted(range(len(blocks)), key=lambda b: (a == 0 and b < 4, b))
                        if a and len(blocks) == 5:
                            pe.wait_ge(tail_made.sem, tail_made.at(L, n - j + 1))
                        for b in order:
                            t0, tn = blocks[b]
                            if b < 4:
                                out = ps[:, 3 * (n % 2) + a, 128 * b:128 * b + 128]
                            else:
                                out = ps[0:64, 3 * (n % 2) + 2, 64 * a:64 * a + 64]
                            ins = pe.matmul(out, k[rows, t0:t0 + tn], q[rows, t0:t0 + tn], start=True, stop=True)
                            if b == 4 and a == 0:
                                ins.then_inc(tail_made.sem, 1)
                    ins.then_inc(A_made.sem, 1)
                    if n == LEVELS:
                        heads(L, 0)
                heads(L, 1)
                pe.wait_ge(O_sq.sem, O_sq.at(L, 1))
                for j in range(2):
                    for c in range(2):
                        ins = pe.matmul(ps[:, 2 * j + c, 0:HALF], head_ones[:, :],
                                        tmp[:, j, c * HALF:(c + 1) * HALF], start=True, stop=True)
                ins.then_inc(O_ms.sem, 1)

            def heads(L, j):
                pe.wait_ge(A_taken.sem, A_taken.at(L, 16 * (j + 1)))
                if j:
                    pe.wait_ge(O_out.sem, O_out.at(L, 2))
                for a in range(2):
                    rows = slice(64 * a, 64 * a + 64)
                    for b, (t0, tn) in enumerate(BLOCKS):
                        out = ps[rows, 6, t0:t0 + tn] if b < 4 else ps[rows, 7, 0:SAMPLE]
                        scores = A[:, a, b, :] if b < 4 else a_tail[:, a, :]
                        ins = pe.matmul(out, V[0:tn, b, 128 * j + 64 * a:128 * j + 64 * a + 64], scores,
                                        start=True, stop=(b == 0))
                        if a and b == 4:
                            ins.then_inc(tail_out.sem, 1)
                            pe.wait_ge(tail_out.sem, tail_out.at(L, j + 1))
                            by_itself(pe)
                        if b:
                            ins = pe.matmul(out, S[rows, j, b if b < 4 else 5, :], qG[rows, j, t0:t0 + tn],
                                            start=False, stop=True)
                ins.then_inc(O_made.sem, 1)

            def attention(L):
                x, un = 0, 0
                pe.wait_ge(O_lo.sem, O_lo.at(L, 1))
                pe.wait_ge(k_placed.sem, k_placed.at(L, 4))
                pe.wait_ge(late_in.sem, late_in.at(L, late_in.per))

                def take_slot(x):
                    pe.wait_ge(s_free[x % 2].sem, L * s_free[x % 2].per + (x // 2 + 1))
                    return 2 * (x % 2)

                for kind in ("swa", "mla"):
                    for pr in range(3):
                        if kind == "mla":
                            wk, wv = ukv_w[:, pr, 0:P], ukv_w[:, pr, P:2 * P]
                            b0 = take_slot(x)
                            for c in range(2):
                                ins = pe.matmul(ps[:, b0 + c, :], wk, ckv[:, 512 * c:512 * c + 512],
                                                start=True, stop=True)
                            ins.then_inc(s_made[x % 2].sem, 1)
                            x += 1
                            b0 = take_slot(x)
                            pe.matmul(ps[:, b0, 0:64], wk, ckv[:, 1024:], start=True, stop=True)
                            pe.matmul(ps[0:64, b0 + 1, 0:P], ckv[:, 1024:], wv, start=True, stop=True) \
                                .then_inc(s_made[x % 2].sem, 1)
                            x += 1
                            b0 = take_slot(x)
                            for t in range(8):
                                ins = pe.matmul(ps[:, b0 + t // 4, 128 * (t % 4):128 * (t % 4) + 128],
                                                ckv[:, 128 * t:128 * t + 128], wv, start=True, stop=True)
                            ins.then_inc(s_made[x % 2].sem, 1)
                            x += 1
                            b0 = take_slot(x)
                            for k in range(2):
                                for c in range(2):
                                    ins = pe.matmul(ps[:, b0 + c, 0:HALF], uq_w[:, k, pr, 0:P],
                                                    cq[:, k, c * HALF:(c + 1) * HALF], start=(k == 0),
                                                    stop=(k == 1))
                            ins.then_inc(s_made[x % 2].sem, 1)
                            rot = x
                            x += 1
                            for a in range(2):
                                b0 = take_slot(x)
                                if a == 0:
                                    pe.wait_ge(s_free[rot % 2].sem, s_free[rot % 2].at(L, rot // 2 + 1))
                                for c in range(2):
                                    pe.matmul(ps[0:96, b0 + c, 0:HALF], comb[:, 1 + a, :],
                                              tq[:, c * HALF:(c + 1) * HALF], start=True, stop=False,
                                              skip_group_check=True)
                                for k in range(2):
                                    for c in range(2):
                                        ins = pe.matmul(ps[0:64, b0 + c, 0:HALF],
                                                        uq_w[:, k, pr, P + 64 * a:P + 64 * a + 64],
                                                        cq[:, k, c * HALF:(c + 1) * HALF], start=False,
                                                        stop=(k == 1), skip_group_check=True)
                                ins.then_inc(s_made[x % 2].sem, 1)
                                x += 1
                            for back in (1, 2):
                                pe.wait_ge(s_free[(x - back) % 2].sem,
                                           s_free[(x - back) % 2].at(L, (x - back) // 2 + 1))
                        x0 = x

                        def scores(v):
                            a, b = divmod(v, 5)
                            t0, nq = BLOCKS[b]
                            b0 = take_slot(x0 + v)
                            if b == 4 and kind == "swa":
                                by_itself(pe)
                            out = ps[:, b0:b0 + 2, :].rearrange("p a n -> p (a n)")
                            if kind == "swa":
                                rows = slice(64 * a, 64 * a + 64)
                                q, keys = swq[rows, pr, t0:t0 + nq], swk
                                k0 = (0, 0, 128, 256, 512)[b]
                            else:
                                rows = slice(0, 96)
                                q, keys = qT[a][rows, t0:t0 + nq], kT[a]
                                k0 = 0 if b < 4 else PROMPT
                            nk = unit_keys(kind, b)
                            late_mask = kind == "mla" and b < 4
                            if nk > 512:
                                pe.matmul(out[0:nq, 0:512], q, keys[rows, k0:k0 + 512], start=True, stop=True)
                                ins = pe.matmul(out[0:nq, 512:nk], q, keys[rows, k0 + 512:k0 + nk],
                                                start=True, stop=True)
                            else:
                                ins = pe.matmul(out[0:nq, 0:nk], q, keys[rows, k0:k0 + nk], start=True,
                                                stop=not late_mask, skip_group_check=late_mask)
                            if late_mask:
                                ins = pe.matmul(out[:, nk - 64:nk], late[0:1, 0:P], late[0:1, P:P + 64],
                                                start=False, stop=True, skip_group_check=True)
                            ins.then_inc(s_made[(x0 + v) % 2].sem, 1)

                        def turn(v):
                            b = v % 5
                            nq = UNIT_Q[b]
                            pe.wait_ge(prob_ready.sem, prob_ready.at(L, un + v + 1))
                            if v >= 2 or un:
                                pe.wait_ge(probT_ready.sem, probT_ready.at(L, un + v - 1))
                            if b == 4:
                                by_itself(pe)
                            for i, t in enumerate(unit_tiles(kind, b)):
                                kn = 64 if b == 4 and i == len(unit_tiles(kind, b)) - 1 else P
                                ins = pe.transpose(ps[0:kn, 4 + v % 2, i * nq:(i + 1) * nq],
                                                   prob[0:nq, v % 2, 128 * i:128 * i + kn], ident[0:nq, 0:nq])
                            ins.then_inc(turned.sem, 1)

                        def weigh(v):
                            a, b = divmod(v, 5)
                            t0, nq = BLOCKS[b]
                            pe.wait_ge(probT_ready.sem, probT_ready.at(L, un + v + 1))
                            if v == 0 and un:
                                pe.wait_ge(att_lo.sem, att_lo.at(L, 2 * (un // 10)))
                            rows = slice(64 * a, 64 * a + 64)
                            out = ps[rows, 6, t0:t0 + nq] if b < 4 else ps[rows, 7, 0:SAMPLE]
                            tiles = unit_tiles(kind, b)
                            for i, t in enumerate(tiles):
                                kn = 64 if b == 4 and i == len(tiles) - 1 else P
                                values = (swv if kind == "swa" else mv)[0:kn, t, 64 * a:64 * a + 64]
                                ins = pe.matmul(out, values, probT[0:kn, v % 2, i * nq:(i + 1) * nq],
                                                start=(i == 0), stop=(i == len(tiles) - 1))
                            ins.then_inc(pv_done.sem, 1)

                        scores(0)
                        scores(1)
                        turn(0)
                        for v in range(10):
                            if v + 2 < 10:
                                scores(v + 2)
                            if v + 1 < 10:
                                turn(v + 1)
                            weigh(v)
                        x += 10
                        un += 10

            pe.wait_ge(const_in.sem, 16 * 9)
            with pe.Fori(0, DEPTH) as L:
                ffn(L, "ffn1")
                mixer_inputs(L)
                hgrn(L)
                attention(L)
                pe.wait_ge(att_lo.sem, att_lo.at(L, 12))
                for m in range(KD):
                    ready(L, CH[f"out{m}"], US[f"out{m}"])
                    dense(CH[f"out{m}"], US[f"out{m}"], hid_hi, hid_lo, KT).then_inc(made.sem, 1)
                ffn(L, "ffn2")
                pe.wait_ge(p_ready.sem, p_ready.at(L, 1))
                for half in range(2):
                    n = CH[f"proj{half}"]
                    for m in range(4):
                        u = US[f"proj{half}.{m}"]
                        ready(L, n, u)
                        dense(n, u, p_hi, p_lo, (0, 1), lambda k, m=m: (2 * m + k) * P).then_inc(made.sem, 1)
                    for m in range(4 * half, 4 * half + 4):
                        u = US[f"gate{m}"]
                        ready(L, CH[f"gate{m}"], u)
                        last = PAD_US if m == KD - 1 else 0
                        dense(CH[f"gate{m}"], u, xg_hi, xg_lo, KT,
                              wait=xg_wait(L * 32 + 25) if m == 0 else None).then_inc(made.sem, 1 + last)
                        if m == 0:
                            norm(L, "ple.norm", L * 32 + 32)
            pe.wait_ge(acc_done.sem, DEPTH * 32 + 8)
            pe.wait_ge(drained.sem, DEPTH * N_US + 1)
            for c in range(2):
                ins = pe.matmul(ps[:, c, 0:HALF], ones[:, :], acc[:, c * HALF:(c + 1) * HALF],
                                start=True, stop=True)
            ins.then_inc(made.sem, 1)


def _chunk(w):
    return w.reshape(-1, P, w.shape[1]).transpose(1, 0, 2).reshape(P, -1)


def _weights(a):
    out = np.zeros((DEPTH * N_CH + AHEAD, P, CHUNK_W), np.float32)
    for i in range(DEPTH):
        def put(name, block):
            out[i * N_CH + CH[name], :, :block.shape[1]] = block

        for f in ("ffn1", "ffn2"):
            up, down = a[f + "_up"][i], a[f + "_down"][i]
            j = 0
            for g, pairs in enumerate(FF_GROUPS):
                for q in range(pairs):
                    put(f"{f}.{g}.up{2 * q}", _chunk(up[:, P * (j + q):P * (j + q + 1)]))
                    put(f"{f}.{g}.up{2 * q + 1}", _chunk(up[:, D_FF + P * (j + q):D_FF + P * (j + q + 1)]))
                for m in range(KD):
                    put(f"{f}.{g}.down{m}", _chunk(down[P * j:P * (j + pairs), P * m:P * (m + 1)]))
                j += pairs
        w = a["w_in"][i]
        mla, swa, hgr = 0, 416, 1056
        kr = w[:, mla + 384:mla + 416]
        swapped = np.concatenate([kr[:, 16:], kr[:, :16]], axis=1)
        cols = {"ckv": w[:, 256:384], "kr": np.concatenate([kr, swapped, kr, swapped], axis=1),
                "swk": w[:, swa + 384:swa + 512], "swv": w[:, swa + 512:swa + 640]}
        for j in range(2):
            cols[f"cq{j}"] = w[:, P * j:P * (j + 1)]
            for s, name in enumerate("qfig"):
                cols[f"{name}{j}"] = w[:, hgr + 256 * s + P * j:hgr + 256 * s + P * (j + 1)]
        for j in range(3):
            cols[f"swq{j}"] = np.concatenate([w[:, swa + 64 * hd:swa + 64 * hd + 64] for hd in (j, j + 3)], axis=1)
        for name, c in cols.items():
            put(name, _chunk(c))
        order = list(range(384))
        for j in range(3):
            for hd in (j, j + 3):
                order += list(range(384 + 64 * hd, 384 + 64 * hd + 64))
        order += list(range(768, 1024))
        wo = a["w_out"][i][order]
        for m in range(KD):
            put(f"out{m}", _chunk(wo[:, P * m:P * (m + 1)]))
            put(f"gate{m}", _chunk(a["ple_gate"][i][:, P * m:P * (m + 1)]))
        for half in range(2):
            put(f"proj{half}", np.concatenate(
                [_chunk(a["ple_proj"][i][:, P * m:P * (m + 1)]) for m in range(4 * half, 4 * half + 4)], axis=1))
    return out


def _rows(v):
    return v.reshape(-1, P).T


def _constants():
    half = ROPE // 2
    inv = np.exp(np.float32(-np.log(10000.0)) * np.arange(half, dtype=np.float32) / np.float32(half)) \
        .astype(np.float32)
    ang = np.arange(TOK, dtype=np.float32)[None, :] * inv[:, None]
    cos, sin = np.cos(ang).astype(np.float32), np.sin(ang).astype(np.float32)
    cos_sin = np.concatenate([cos, cos, -sin, sin] * 2, axis=0)
    comb = np.zeros((P, 3, 96), np.float32)
    for i in range(ROPE):
        for a, first in ((0, 0), (1, 0), (2, 64)):
            comb[first + i, a, 64 + i] = comb[first + 32 + i, a, 64 + i] = 1
    head_ones = np.kron(np.eye(2), np.full((64, 64), 1 / 64)).astype(np.float32)
    q, k = np.arange(P)[:, None], np.arange(256)[None, :]
    back = (q + 128) // 64 - k // 64
    dist = np.where((back >= 0) & (back <= 2), np.abs(q + 128 - k), FAR).astype(np.float32)
    s, t = np.arange(P)[:, None], np.arange(P)[None, :]
    mask = np.zeros((P, LEVELS - 1, P), np.float32)
    for lv in range(1, LEVELS):
        m = 1 << lv
        mask[:, lv - 1] = (s // m == t // m) & (s % m < m // 2) & (t % m >= m // 2)
    late = np.zeros((1, P + 64), np.float32)
    late[0, :64] = 1
    late[0, P:] = NEG
    return dict(cos_sin=cos_sin, ident_d=np.eye(P, dtype=np.float32),
                ones_d=np.full((P, P), 1 / D_MODEL, np.float32), head_ones_d=head_ones, comb_d=comb,
                dist_d=dist, mask_d=mask, late_d=late)


def kernel(**inputs):
    import concourse.bacc as bacc
    from concourse.bass_utils import run_bass_kernel_spmd

    a = {k: np.asarray(v) for k, v in inputs.items()}

    def tokens(prompt, sample):
        both = np.concatenate([prompt, sample], axis=0).T
        return both.reshape(-1, P, TOK).transpose(1, 0, 2)

    par = np.zeros((DEPTH + 1, P, PAR_W), np.float32)
    par[DEPTH, :, PAR["next"]:PAR["next"] + KD] = _rows(a["ffn1_norm"][0])
    uq = np.zeros((DEPTH, P, 2, 3, 256), np.float32)
    ukv = np.zeros((DEPTH, P, 3, 256), np.float32)
    for i in range(DEPTH):
        following = a["ffn1_norm"][i + 1] if i + 1 < DEPTH else a["final_norm"]
        for key, v in (("mix", a["mix_norm"][i]), ("ffn2", a["ffn2_norm"][i]), ("ple", a["ple_norm"][i]),
                       ("next", following), ("q_norm", a["mla_q_norm"][i]), ("kv_norm", a["mla_kv_norm"][i]),
                       ("hg_out", np.concatenate([a["hg_out_norm"][i]] * 2))):
            par[i, :, PAR[key]:PAR[key] + v.size // P] = _rows(v)
        par[i, :, PAR["sink"]:PAR["sink"] + 6] = a["swa_sinks"][i][None, :]
        wq = a["mla_w_uq"][i].reshape(2, P, 6, 96).transpose(1, 0, 2, 3)
        wkv = a["mla_w_ukv"][i].reshape(P, 6, 128)
        for pr in range(3):
            for e in range(2):
                hd = wq[:, :, 2 * pr + e]
                rot = hd[:, :, 64:]
                uq[i, :, :, pr, 64 * e:64 * e + 32] = rot
                uq[i, :, :, pr, 64 * e + 32:64 * e + 64] = np.concatenate([rot[..., 16:], rot[..., :16]], axis=-1)
                uq[i, :, :, pr, 128 + 64 * e:192 + 64 * e] = hd[:, :, :64]
                ukv[i, :, pr, 64 * e:64 * e + 64] = wkv[:, 2 * pr + e, :64]
                ukv[i, :, pr, 128 + 64 * e:192 + 64 * e] = wkv[:, 2 * pr + e, 64:]

    c = _constants()
    feed = dict(
        x_t=tokens(a["x_prompt"][0], a["x_sample"][0]),
        p_t=np.stack([tokens(a["p_prompt"][i, 0], a["p_sample"][i, 0]) for i in range(DEPTH)]),
        w_all=_weights(a), uq=uq, ukv=ukv, par_d=par,
        logits_d=np.stack([_rows(a["hg_lb_logits"][i]) for i in range(DEPTH)], axis=1),
        cos_sin=c["cos_sin"], ident_d=c["ident_d"], ones_d=c["ones_d"], head_ones_d=c["head_ones_d"],
        comb_d=c["comb_d"], dist_d=c["dist_d"], mask_d=c["mask_d"], late_d=c["late_d"],
        ckv_c=a["cache_mla_ckv"][:, 0].transpose(0, 2, 1), krope_c=a["cache_mla_krope"][:, 0].transpose(0, 2, 1),
        swk_c=a["cache_swa_k"][:, 0].reshape(DEPTH, 128, 128).transpose(0, 2, 1),
        swv_c=a["cache_swa_v"][:, 0].reshape(DEPTH, 128, 128),
        hg_s=a["state_hgrn"][:, 0].reshape(DEPTH, 2, P, 64).transpose(0, 2, 1, 3),
    )
    outs = dict(y_t=(P, KD, TOK), ckv_o=(DEPTH, P, TOK), krope_o=(DEPTH, ROPE, TOK),
                swk_o=(DEPTH, 2, P, P), swv_o=(DEPTH, 2, P, P), hg_o=(DEPTH, 2, P, 2, 64))
    nc = bacc.Bacc("TRN2", target_bir_lowering=False, num_devices=1)
    feed = {k: np.ascontiguousarray(v) for k, v in feed.items()}
    args = {k: nc.dram_tensor(k, v.shape, mybir.dt.from_np(v.dtype), kind="ExternalInput").ap()
            for k, v in feed.items()}
    args |= {k: nc.dram_tensor(k, s, F32, kind="ExternalOutput").ap() for k, s in outs.items()}
    hybrid_step(nc, **args)
    res = run_bass_kernel_spmd(nc, [feed], core_ids=[0]).results[0]

    y = res["y_t"].transpose(2, 1, 0).reshape(TOK, D_MODEL)
    ckv = res["ckv_o"].transpose(0, 2, 1)
    krope = res["krope_o"].transpose(0, 2, 1)
    swk = res["swk_o"].transpose(0, 1, 3, 2).reshape(DEPTH, 2, 1, 128, 2, 64)
    swv = res["swv_o"].reshape(DEPTH, 2, 1, 128, 2, 64)
    hgs = res["hg_o"].transpose(0, 1, 3, 2, 4).reshape(DEPTH, 2, 1, 4, 64, 64)
    c = np.ascontiguousarray
    return (c(y[None, :PROMPT]), c(y[None, PROMPT:]),
            c(ckv[:, None, :PROMPT]), c(krope[:, None, :PROMPT]), c(swk[:, 0]), c(swv[:, 0]), c(hgs[:, 0]),
            c(ckv[:, None, PROMPT:]), c(krope[:, None, PROMPT:]), c(swk[:, 1]), c(swv[:, 1]), c(hgs[:, 1]))
```

```python
from contextlib import ExitStack

import numpy as np

import concourse.bass as bass
from concourse import mybir

F32 = mybir.dt.float32
F32R = mybir.dt.float32r
U8 = mybir.dt.uint8
ALU = mybir.AluOpType
ACT = mybir.ActivationFunctionType
AX = mybir.AxisListType

P = 128
DEPTH, D_MODEL, D_FF = 2, 1024, 2816
PROMPT, SAMPLE, PAST = 512, 64, 512
TOK = PROMPT + SAMPLE
HALF = TOK // 2
KD = D_MODEL // P
EPS, TINY = 1e-6, 1e-30
CHUNK_W = KD * P
FF_GROUPS = (8, 8, 6)
ROPE, NOPE = 32, 64
MLA_SCALE = (NOPE + ROPE) ** -0.5
SWA_SCALE = 64 ** -0.5
NEG = -1e30
FAR = 1e33
W_SLOTS, RAW_SLOTS, AHEAD = 4, 2, 3
LEVELS = 8
BLOCKS = ((0, 128), (128, 128), (256, 128), (384, 128), (512, 64))

W_IN = ("f0", "f1", "q0", "q1", "g0", "g1", "i0", "i1", "ckv", "kr", "cq0", "cq1", "swk", "swv",
        "swq0", "swq1", "swq2", "spare")
PAR = dict(mix=0, ffn2=8, ple=16, next=24, q_norm=32, kv_norm=34, hg_out=35, sink=36)
PAR_W = 42


def plan():
    chunks, uses, last_use = {}, {}, []

    def use(name):
        uses[name] = len(uses)

    def chunk(name, *made):
        chunks[name] = len(chunks)
        for m in made or (name,):
            use(m)
        last_use.append(len(uses) - 1)

    def ffn(f):
        for g, pairs in enumerate(FF_GROUPS):
            for q in range(2 * pairs):
                chunk(f"{f}.{g}.up{q}")
                if g == 0 and q == 1:
                    use(f"{f}.norm")
            for m in range(KD):
                chunk(f"{f}.{g}.down{m}")

    ffn("ffn1")
    for name in W_IN:
        if name == "spare":
            chunks[name] = len(chunks)
            last_use.append(len(uses) - 1)
            continue
        chunk(name)
        if name == "f1":
            use("mix.norm")
        if name == "cq1":
            use("ckv.norm")
        if name == "swk":
            use("kr.sum")
            use("cq.norm")
    for m in range(KD):
        chunk(f"out{m}")
    ffn("ffn2")
    for half in range(2):
        chunk(f"proj{half}", *(f"proj{half}.{m}" for m in range(4)))
        for m in range(4):
            chunk(f"gate{4 * half + m}")
            if half == 0 and m == 0:
                use("ple.norm")
    assert len(chunks) % W_SLOTS == 0
    return chunks, uses, last_use


CH, US, LAST = plan()
N_CH = len(CH)
PAD_US = -len(US) % 4
N_US = len(US) + PAD_US


UNITS, PAIR_UNITS, PROJECTIONS = 60, 10, 6
HEAD_HI = 8
UNIT_Q = (P, P, P, P, SAMPLE)

def unit_keys(kind, b):
    if kind == "swa":
        return (128, 256, 256, 256, 192)[b]
    return (128, 256, 384, 512, PAST + SAMPLE)[b]

def unit_tiles(kind, b):
    if kind == "swa":
        return ((0,), (0, 1), (1, 2), (2, 3), (4, 5))[b]
    return ((0,), (0, 1), (0, 1, 2), (0, 1, 2, 3), (4, 5, 6, 7, 8))[b]


def unit(u):
    pair, v = divmod(u, PAIR_UNITS)
    kind = "swa" if pair < 3 else "mla"
    return kind, pair % 3, v, u + PROJECTIONS * max(0, pair - 2) + max(0, (u - 3) // PAIR_UNITS)


def out_use(u):
    return unit(u + 3)[3] - 1 if u < UNITS else unit(UNITS - 1)[3] + 1


def out_tile(u):
    return (u // PAIR_UNITS + 3) % 6


def opens_mla_pair(u):
    return u < UNITS and u % PAIR_UNITS == 0 and u // PAIR_UNITS >= 3


class Event:

    def __init__(self, ctx, nc, name, per, seed=0):
        self.sem = ctx.enter_context(nc.semaphore(name))
        self.per, self.seed = per, seed

    def at(self, layer, count, more=0):
        return layer * self.per + (count + self.seed) + more


def hybrid_step(nc, x_t, p_t, w_all, uq, ukv, par_d, logits_d, cos_sin, ident_d, ones_d, head_ones_d, comb_d,
                dist_d, mask_d, late_d, ckv_c, krope_c, swk_c, swv_c, hg_s,
                y_t, ckv_o, krope_o, swk_o, swv_o, hg_o):
    ctx = ExitStack()
    with ctx:
        base = -(-nc.sbuf_base // 64) * 64
        top = [base]

        def place(name, shape, dt=F32, at=None):
            size = int(np.prod(shape[1:])) * (1 if dt == U8 else 4)
            offset = top[0] if at is None else at
            if at is None:
                top[0] += -(-size // 32) * 32
            return nc.alloc_sbuf_tensor_at(name, shape, dt, offset=offset)

        T_BYTES = TOK * 4
        h = place("h", [P, KD, TOK])
        xg_at = top[0]
        xg_hi = place("xg_hi", [P, KD, TOK], F32R)
        xg_lo = place("xg_lo", [P, KD, TOK], F32R)
        xg_end = top[0]
        hid_at = top[0]
        hid_hi = place("hid_hi", [P, KD, TOK], F32R)
        hid_lo_at = top[0]
        hid_lo = place("hid_lo", [P, KD, TOK], F32R)
        w_raw = place("w_raw", [P, RAW_SLOTS, CHUNK_W])
        w_hi = place("w_hi", [P, W_SLOTS, CHUNK_W], F32R)
        w_lo = place("w_lo", [P, W_SLOTS, CHUNK_W], F32R)
        r = place("r", [P, TOK])
        r_col = place("r_col", [P, 5])
        acc = place("acc", [P, TOK])
        sq = place("sq", [P, TOK])
        par = place("par", [P, PAR_W])
        cs = place("cs", [P, TOK])
        ident = place("ident", [P, P])
        ones = place("ones", [P, P])
        head_ones = place("head_ones", [P, P])
        comb = place("comb", [P, 3, 96])
        dist = place("dist", [P, 256])
        mask = place("mask", [P, LEVELS - 1, P], U8)
        late = place("late", [1, P + 64])
        eps = place("eps", [P, 1])
        lbl = place("lbl", [P, DEPTH, 2])
        lbt = place("lbt", [P, 4, 2])
        lb = place("lb", [P, 2])
        lb_next = place("lb_next", [P, 2])
        one_minus_lb = place("one_minus_lb", [P, 2])
        no_sink = place("no_sink", [P, 6])
        p_raw = place("p_raw", [P, 2, TOK])
        dense_at = top[0]
        G = place("G", [P, 2, TOK])
        hk = place("hk", [P, 2, TOK])
        hq = place("hq", [P, 2, TOK])
        hg = place("hg", [P, 2, TOK])
        gate = place("gate", [P, 2, TOK], at=dense_at)
        val = place("val", [P, 2, TOK], at=dense_at + 2 * T_BYTES)
        mv = [place(f"mv{i}", [P, 9, P], at=dense_at + 2 * (i + 1) * T_BYTES) for i in range(2)]
        o_tok = place("o_tok", [P, 2, 5, P], at=dense_at)
        p_hi = place("p_hi", [P, 2, TOK], F32R, at=dense_at + 4 * T_BYTES)
        p_lo = place("p_lo", [P, 2, TOK], F32R, at=dense_at + 6 * T_BYTES)
        V = place("V", [P, 5, 256])
        S = place("S", [P, 2, 7, 64])
        a_tail = place("a_tail", [64, 2, 64])
        e_end = place("e_end", [P, 2, 5])
        swq = place("swq", [P, 3, TOK])
        swk = place("swk", [P, PROMPT + 128 + SAMPLE])
        swv = place("swv", [P, 6, P])
        cq = place("cq", [P, 2, TOK])
        ckv = place("ckv", [P, PROMPT + PAST + SAMPLE])
        krs = place("krs", [P, TOK])
        uq_w = place("uq_w", [P, 2, 3, 256])
        assert top[0] <= nc.sbuf_usable_end, (top[0], nc.sbuf_usable_end)
        tmp = place("tmp", [P, 6, TOK], at=hid_at)
        eG = place("eG", [P, 2, TOK], at=hid_at + 6 * T_BYTES)
        kd = place("kd", [P, 2, TOK], at=hid_lo_at + 6 * T_BYTES)
        mask_f = place("mask_f", [P, LEVELS - 1, P], at=hid_at)
        qG = place("qG", [P, 2, TOK], at=hid_lo_at)
        kdT = place("kdT", [P, 2, 5, P], at=hid_lo_at + 2 * T_BYTES)
        fx = place("fx", [P, 2, TOK], at=hid_lo_at + 2 * T_BYTES)
        A = place("A", [P, 2, 4, P], at=hid_lo_at + 2 * T_BYTES + 5120)
        pp = place("pp", [P, 4, TOK], at=hid_at)
        y = place("y", [P, KD, TOK], at=hid_at)
        off = [xg_at]

        def over(name, shape):
            t = place(name, shape, at=off[0])
            off[0] += -(-int(np.prod(shape[1:])) * 4 // 32) * 32
            assert off[0] <= xg_end
            return t

        kT = [over(f"kT{a}", [P, PROMPT + PAST + SAMPLE]) for a in range(2)]
        qT = [over(f"qT{a}", [P, TOK]) for a in range(2)]
        tq = over("tq", [P, TOK])
        prob = over("prob", [P, 2, TOK])
        probT = over("probT", [P, 2, PROMPT])
        score = over("score", [P, 2, 256])
        stat = over("stat", [P, 2, 6])
        ukv_w = over("ukv_w", [P, 3, 256])

        ps = ctx.enter_context(nc.psum_tensor("ps", [P, 8, 512], F32))

        def slot(u):
            return ps[:, 2 * (u % 4):2 * (u % 4) + 2, 0:HALF]

        def bank(u):
            return 2 * (u % 4)

        def halves(ap):
            return ap.rearrange("p (a n) -> p a n", a=2)

        def ev(name, per, seed=0):
            return Event(ctx, nc, name, per, seed)

        raw_in = [ev(f"raw_in{s}", 16 * N_CH // RAW_SLOTS) for s in range(RAW_SLOTS)]
        whi_ready = ev("whi_ready", N_CH)
        wlo_ready = ev("wlo_ready", N_CH, RAW_SLOTS)
        made = ev("made", N_US, 8)
        drained = ev("drained", N_US, 4)
        silu_done = ev("silu_done", 44)
        prod_done = ev("prod_done", 44)
        hidhi_ready = ev("hidhi_ready", 44)
        hid_ready = ev("hid_ready", 44)
        xhi_ready = ev("xhi_ready", 32, 8)
        xg_ready = ev("xg_ready", 32, 8)
        sq_done = ev("sq_done", 28, 7)
        acc_done = ev("acc_done", 32, 8)
        root_done = ev("root_done", 7)
        inverted = ev("inverted", 4)
        passed = ev("passed", 0)
        const_in = ev("const_in", 0)
        x_in = ev("x_in", 0)
        lb_step = ev("lb_step", 0)
        lb_exp = ev("lb_exp", 0)
        layer_in = ev("layer_in", 16 * 7)
        late_in = ev("late_in", 16 * 3)
        silu_in = ev("silu_in", 2)
        c_raw = ev("c_raw", 1)
        c_sq = ev("c_sq", 3)
        c_norm = ev("c_norm", 7)
        f_exp = ev("f_exp", 1)
        f_step = ev("f_step", 8)
        f_ln = ev("f_ln", 1)
        G_ready = ev("G_ready", 10)
        eG_ready = ev("eG_ready", 1)
        qG_ready = ev("qG_ready", 3)
        kd_diff = ev("kd_diff", 3)
        kd_exp = ev("kd_exp", 1)
        kd_ready = ev("kd_ready", 1)
        kd_turned = ev("kd_turned", 1)
        kdT_ready = ev("kdT_ready", 4)
        dS_made = ev("dS_made", 1)
        S_ready = ev("S_ready", 10)
        lv_diff = ev("lv_diff", 28)
        lv_exp = ev("lv_exp", 14)
        lv_qk = ev("lv_qk", 28)
        A_made = ev("A_made", 16)
        tail_made = ev("tail_made", 14)
        tail_out = ev("tail_out", 2)
        A_taken = ev("A_taken", 32)
        O_made = ev("O_made", 2)
        O_out = ev("O_out", 4)
        O_sq = ev("O_sq", 1)
        O_ms = ev("O_ms", 1)
        O_root = ev("O_root", 2)
        O_norm = ev("O_norm", 4)
        O_hi = ev("O_hi", 1)
        O_lo = ev("O_lo", 1)
        k_placed = ev("k_placed", 4)
        s_uses = (UNITS + 3 * PROJECTIONS + UNITS // PAIR_UNITS) // 2
        s_made = [ev(f"s_made{i}", s_uses) for i in range(2)]
        s_free = [ev(f"s_free{i}", s_uses, 1) for i in range(2)]
        scored = ev("scored", 60)
        bound_done = ev("bound_done", 60)
        exp_done = ev("exp_done", 30)
        sink_done = ev("sink_done", 30)
        den_done = ev("den_done", 30)
        recip_done = ev("recip_done", 60)
        o_taken = ev("o_taken", 60)
        turned = ev("turned", 60)
        probT_ready = ev("probT_ready", 60)
        pv_done = ev("pv_done", 60)
        att_hi = ev("att_hi", 6)
        p_split = ev("p_split", 1)
        p_ready = ev("p_ready", 1)
        sig_done = ev("sig_done", 8)
        emb_mul = ev("emb_mul", 8)
        h_emb = ev("h_emb", 8)
        y_done = ev("y_done", 0)
        stored = ev("stored", 16 * 10)

        block = ctx.enter_context(nc.Block())

        def exp_wait(engine, layer, u):
            kind, _, _, x = unit(u)
            if kind == "swa":
                engine.wait_ge(exp_done.sem, exp_done.at(layer, u + 1))
            else:
                engine.wait_ge(s_free[x % 2].sem, s_free[x % 2].at(layer, x // 2 + 1))

        def by_itself(engine):
            engine.sem_inc(passed.sem, 1)

        UP = [(f, g, pairs) for f in ("ffn1", "ffn2") for g, pairs in enumerate(FF_GROUPS)]

        def hid_before(f, g):
            return sum(FF_GROUPS[:g]) + (22 if f == "ffn2" else 0)

        @block.sync
        def _(sp):
            def load(layer, n, count):
                assert n % RAW_SLOTS == 0 and count % RAW_SLOTS == 0
                with sp.Fori(0, count // RAW_SLOTS) as i:
                    for s in range(RAW_SLOTS):
                        sp.wait_ge(wlo_ready.sem, layer * N_CH + (n + s + 1) + i * RAW_SLOTS)
                        sp.dma_start(w_raw[:, s, :], w_all[layer * N_CH + (n + s) + i * RAW_SLOTS]) \
                          .then_inc(raw_in[s].sem, 16)

            with sp.Fori(0, DEPTH) as L:
                load(L, 0, 16)
                sp.wait_ge(xg_ready.sem, xg_ready.at(L, 0))
                sp.dma_start(par[:, :], par_d[L]).then_inc(layer_in.sem, 16)
                sp.dma_start(uq_w[:, :, :, :], uq[L]).then_inc(layer_in.sem, 16)
                sp.dma_start(ckv[:, PROMPT:PROMPT + PAST], ckv_c[L]).then_inc(layer_in.sem, 16)
                sp.dma_start(swk[:, PROMPT:PROMPT + 128], swk_c[L]).then_inc(layer_in.sem, 16)
                sp.dma_start(swv[:, 4, :], swv_c[L]).then_inc(layer_in.sem, 16)
                sp.dma_start(S[:, :, 5, :], hg_s[L]).then_inc(layer_in.sem, 16)
                sp.dma_start(p_raw[:, :, :], p_t[L]).then_inc(layer_in.sem, 16)
                n_mix = CH["out2"] + 1 + (CH["out2"] + 1) % 2
                load(L, 16, n_mix - 16)
                sp.wait_ge(made.sem, made.at(L, US["swq2"] + 1))
                sp.dma_start(kT[0][64:96, PROMPT:PROMPT + PAST], krope_c[L]).then_inc(late_in.sem, 16)
                sp.dma_start(kT[1][64:96, PROMPT:PROMPT + PAST], krope_c[L]).then_inc(late_in.sem, 16)
                sp.dma_start(ukv_w[:, :, :], ukv[L]).then_inc(late_in.sem, 16)
                sp.wait_ge(c_norm.sem, c_norm.at(L, 7))
                sp.dma_start(ckv_o[L, :, 0:PROMPT], ckv[:, 0:PROMPT]).then_inc(stored.sem, 16)
                sp.dma_start(ckv_o[L, :, PROMPT:TOK], ckv[:, PROMPT + PAST:]).then_inc(stored.sem, 16)
                sp.dma_start(krope_o[L], krs[64:96, :]).then_inc(stored.sem, 16)
                sp.wait_ge(drained.sem, drained.at(L, US["swq2"] + 1))
                sp.dma_start(swk_o[L, 0], swk[:, PROMPT - 128:PROMPT]).then_inc(stored.sem, 16)
                sp.dma_start(swk_o[L, 1], swk[:, PROMPT + 64:]).then_inc(stored.sem, 16)
                sp.dma_start(swv_o[L, 0], swv[:, 3, :]).then_inc(stored.sem, 16)
                sp.dma_start(swv_o[L, 1, 0:64], swv[64:128, 4, :]).then_inc(stored.sem, 16)
                sp.dma_start(swv_o[L, 1, 64:128], swv[0:64, 5, :]).then_inc(stored.sem, 16)
                sp.wait_ge(S_ready.sem, S_ready.at(L, 10))
                sp.dma_start(hg_o[L, 0], S[:, :, 4, :]).then_inc(stored.sem, 16)
                sp.dma_start(hg_o[L, 1], S[:, :, 6, :]).then_inc(stored.sem, 16)
                sp.wait_ge(stored.sem, stored.at(L, stored.per))
                by_itself(sp)
                load(L, n_mix, N_CH - n_mix)
            for n in range(AHEAD):
                sp.wait_ge(wlo_ready.sem, DEPTH * N_CH + n + 1)
                sp.dma_start(w_raw[:, n % RAW_SLOTS, :], w_all[DEPTH * N_CH + n]) \
                  .then_inc(raw_in[n % RAW_SLOTS].sem, 16)
            for t in range(KD):
                sp.wait_ge(y_done.sem, t + 1)
                sp.dma_start(y_t[:, t, :], y[:, t, :]).then_inc(stored.sem, 16)
            sp.wait_ge(stored.sem, DEPTH * stored.per + 16 * KD)

        @block.scalar
        def _(act):
            act.dma_start(h[:, :, :], x_t).then_inc(x_in.sem, 16)
            act.dma_start(par[:, :], par_d[DEPTH]).then_inc(x_in.sem, 16)
            for dst, src in ((cs[:, :], cos_sin), (ident[:, :], ident_d), (ones[:, :], ones_d),
                             (head_ones[:, :], head_ones_d), (comb[:, :, :], comb_d), (dist[:, :], dist_d),
                             (mask_f[:, :, :], mask_d), (late[:, :], late_d), (lbl[:, :, :], logits_d)):
                act.dma_start(dst, src).then_inc(const_in.sem, 16)

            def split_hi(layer, n, more=0):
                s = n % W_SLOTS
                act.wait_ge(raw_in[n % RAW_SLOTS].sem,
                            layer * raw_in[0].per + 16 * (n // RAW_SLOTS + 1) + more * (16 * 4 // RAW_SLOTS))
                free = LAST[n - 4] + 1 if n >= 4 else LAST[N_CH + n - 4] + 1 - len(US) - PAD_US
                act.wait_ge(made.sem, layer * N_US + (free + made.seed) + more * 4)
                act.activation(w_hi[:, s, :], w_raw[:, n % RAW_SLOTS, :], ACT.Copy).then_inc(whi_ready.sem, 1)

            def step(layer, n, more=0):
                split_hi(layer, n + AHEAD, more) if n + AHEAD < N_CH else split_hi(layer + 1, n + AHEAD - N_CH, more)

            def root(layer, use, scale, out, k):
                act.wait_ge(made.sem, made.at(layer, US[use] + 1))
                act.activation(halves(out), slot(US[use]), ACT.Sqrt, bias=eps[:, 0:1], scale=scale) \
                   .then_inc(root_done.sem, 1)
                if use == "mix.norm":
                    act.activation(r_col[:, 0:4], ps[:, bank(US[use]), 400:404], ACT.Sqrt, bias=eps[:, 0:1])
                    act.activation(r_col[0:64, 4:5], ps[0:64, bank(US[use]), 404:405], ACT.Sqrt,
                                   bias=eps[0:64, 0:1]) \
                       .then_inc(root_done.sem, 1)

            def xg_split(t, gain):
                act.activation(xg_hi[:, t, :], h[:, t, :], ACT.Copy, scale=par[:, gain + t:gain + t + 1]) \
                   .then_inc(xhi_ready.sem, 1)

            act.wait_ge(x_in.sem, 32)
            for t in range(KD):
                xg_split(t, PAR["next"])
            for n in range(AHEAD):
                split_hi(0, n)
            act.wait_ge(lb_step.sem, 3)
            act.activation(lbt[:, 1:3, :], lbt[:, 1:3, :], ACT.Exp).then_inc(lb_exp.sem, 1)

            def ffn(L, f):
                for g, pairs in enumerate(FF_GROUPS):
                    c0, u0 = CH[f"{f}.{g}.up0"], US[f"{f}.{g}.up0"]
                    j0 = hid_before(f, g)

                    def two_pairs(i, c, u, tile, first):
                        for pr in range(2):
                            step(L, c + 2 * pr, i)
                            if first and pr == 0:
                                step(L, c + 1, i)
                                root(L, f"{f}.norm", 1.0, r[:, :], 0)
                            ug = u + 2 * pr + (1 if first and pr else 0)
                            act.wait_ge(drained.sem, drained.at(L, ug + 1, i * 4))
                            act.activation(gate[:, pr, :], gate[:, pr, :], ACT.Silu).then_inc(silu_done.sem, 1)
                            if not (first and pr == 0):
                                step(L, c + 2 * pr + 1, i)
                            act.wait_ge(prod_done.sem, prod_done.at(L, j0 + tile + pr + 1, i * 2))
                            act.activation(hid_hi[:, tile + pr + i * 2, :], val[:, pr, :], ACT.Copy) \
                               .then_inc(hidhi_ready.sem, 1)

                    if g == 0:
                        two_pairs(0, c0, u0, 0, True)
                        with act.Fori(0, pairs // 2 - 1) as i:
                            two_pairs(i, c0 + 4, u0 + 5, 2, False)
                    else:
                        with act.Fori(0, pairs // 2) as i:
                            two_pairs(i, c0, u0, 0, False)
                    d0, v0 = CH[f"{f}.{g}.down0"], US[f"{f}.{g}.down0"]
                    if g < len(FF_GROUPS) - 1:
                        with act.Fori(0, KD // 4) as i:
                            for q in range(4):
                                step(L, d0 + q, i)
                        continue
                    for m in range(KD):
                        step(L, d0 + m)
                        act.wait_ge(drained.sem, drained.at(L, v0 + m + 1))
                        if f == "ffn1" and m == 0:
                            act.wait_ge(layer_in.sem, layer_in.at(L, layer_in.per))
                        xg_split(m, PAR["mix"] if f == "ffn1" else PAR["ple"])

            def mixer_inputs(L):
                for name in W_IN:
                    step(L, CH[name])
                    if name == "f1":
                        root(L, "mix.norm", 1.0, r[:, :], 0)
                    if name == "q1":
                        act.wait_ge(drained.sem, drained.at(L, US["f1"] + 1))
                        act.activation(fx[:, :, :], fx[:, :, :], ACT.Exp, scale=-1.0).then_inc(f_exp.sem, 1)
                    if name == "i1":
                        act.wait_ge(f_step.sem, f_step.at(L, 7))
                        act.activation(fx[:, :, :], fx[:, :, :], ACT.Ln).then_inc(f_ln.sem, 1)
                    if name == "kr":
                        act.wait_ge(G_ready.sem, G_ready.at(L, 10))
                        act.activation(eG[:, :, :], G[:, :, :], ACT.Exp).then_inc(eG_ready.sem, 1)
                        act.wait_ge(kd_diff.sem, kd_diff.at(L, 3))
                        act.activation(kd[:, :, :], kd[:, :, :], ACT.Exp).then_inc(kd_exp.sem, 1)
                    if name == "g0":
                        act.wait_ge(drained.sem, drained.at(L, US["q1"] + 1))
                        act.activation(hq[:, :, :], hq[:, :, :], ACT.Silu).then_inc(silu_in.sem, 1)
                    if name == "i0":
                        act.wait_ge(drained.sem, drained.at(L, US["g1"] + 1))
                        act.activation(hg[:, :, :], hg[:, :, :], ACT.Silu).then_inc(silu_in.sem, 1)
                    if name == "swk":
                        root(L, "ckv.norm", D_MODEL / 128, tmp[:, 5, :], 0)
                    if name == "swv":
                        root(L, "cq.norm", D_MODEL / 256, tmp[:, 1, :], 0)

            def hgrn(L):
                act.wait_ge(kd_turned.sem, kd_turned.at(L, 1))
                for j in range(2):
                    act.activation(kdT[:, j, 0:4, :], ps[:, 2 * j, :].rearrange("p (b k) -> p b k", b=4),
                                   ACT.Copy).then_inc(kdT_ready.sem, 1)
                    act.activation(kdT[0:64, j, 4, :], ps[0:64, 2 * j + 1, 0:P], ACT.Copy) \
                       .then_inc(kdT_ready.sem, 1)
                for n in range(2 * LEVELS):
                    j, lv = divmod(n, LEVELS)
                    if lv:
                        width = PROMPT if lv == LEVELS - 1 else TOK
                        act.wait_ge(lv_diff.sem, lv_diff.at(L, 2 * (n - j)))
                        act.activation(tmp[:, n % 2, 0:width], tmp[:, n % 2, 0:width], ACT.Exp) \
                           .then_inc(lv_exp.sem, 1)
                    if n == LEVELS + 2:
                        head_out(L, 0)
                head_out(L, 1)
                act.wait_ge(O_out.sem, O_out.at(L, 4))
                act.activation(tmp[:, 0:2, :], hk[:, :, :], ACT.Square).then_inc(O_sq.sem, 1)

            def head_out(L, j):
                act.wait_ge(O_made.sem, O_made.at(L, j + 1))
                act.wait_ge(lv_qk.sem, lv_qk.at(L, 14 * (j + 1)))
                act.activation(hk[:, j, 0:PROMPT], ps[:, 6, :], ACT.Copy, scale=0.125).then_inc(O_out.sem, 1)
                act.activation(hk[:, j, PROMPT:], ps[:, 7, 0:SAMPLE], ACT.Copy, scale=0.125) \
                   .then_inc(O_out.sem, 1)

            def s_flat(x):
                return ps[:, 2 * (x % 2):2 * (x % 2) + 2, :].rearrange("p a n -> p (a n)")

            def project(L, u):
                x = unit(u)[3] - PROJECTIONS
                act.wait_ge(s_made[x % 2].sem, s_made[x % 2].at(L, x // 2 + 1))
                act.activation(kT[0][0:64, 0:1024], s_flat(x)[0:64, :], ACT.Copy)
                act.activation(kT[1][0:64, 0:1024], s_flat(x)[64:P, :], ACT.Copy) \
                   .then_inc(s_free[x % 2].sem, 1)
                x += 2
                values = mv[unit(u)[1] % 2]
                act.wait_ge(s_made[x % 2].sem, s_made[x % 2].at(L, x // 2 + 1))
                for a in range(2):
                    act.activation(kT[a][0:64, 1024:], ps[64 * a:64 * a + 64, 2 * (x % 2), 0:64], ACT.Copy)
                act.activation(values[0:64, 8, :], ps[0:64, 2 * (x % 2) + 1, 0:P], ACT.Copy) \
                   .then_inc(s_free[x % 2].sem, 1)
                x += 2
                act.wait_ge(s_made[x % 2].sem, s_made[x % 2].at(L, x // 2 + 1))
                act.activation(values[:, 0:8, :].rearrange("p (a t) v -> p a (t v)", a=2),
                               ps[:, 2 * (x % 2):2 * (x % 2) + 2, :], ACT.Copy).then_inc(s_free[x % 2].sem, 1)

            def softmax_exp(L, u):
                kind, pr, v, x = unit(u)
                b = u % 2
                nq, nk = UNIT_Q[v % 5], unit_keys(kind, v % 5)
                act.wait_ge(bound_done.sem, bound_done.at(L, u + 1))
                if u >= 2:
                    act.wait_ge(turned.sem, turned.at(L, u - 1))
                src = score[0:nq, b, 0:nk] if kind == "swa" else s_flat(x)[0:nq, 0:nk]
                act.activation(prob[0:nq, b, 0:nk], src, ACT.Exp, bias=stat[0:nq, b, 1:2],
                               scale=SWA_SCALE if kind == "swa" else MLA_SCALE,
                               accum_out=stat[0:nq, b, 2:3]) \
                   .then_inc(exp_done.sem if kind == "swa" else s_free[x % 2].sem, 1)
                if kind == "swa":
                    hd = pr + 3 * (v // 5)
                    act.activation(stat[0:nq, b, 3:4], par[0:nq, PAR["sink"] + hd:PAR["sink"] + hd + 1],
                                   ACT.Exp, bias=stat[0:nq, b, 1:2]).then_inc(sink_done.sem, 1)

            def copy_t(L, u):
                kind, _, v, _ = unit(u)
                tiles, nq = unit_tiles(kind, v % 5), UNIT_Q[v % 5]
                act.wait_ge(turned.sem, turned.at(L, u + 1))
                if u >= 2:
                    act.wait_ge(pv_done.sem, pv_done.at(L, u - 1))
                full = len(tiles) - (1 if v % 5 == 4 else 0)
                if full < len(tiles):
                    act.activation(probT[0:64, u % 2, full * nq:(full + 1) * nq],
                                   ps[0:64, 4 + u % 2, full * nq:(full + 1) * nq], ACT.Copy)
                act.activation(probT[:, u % 2, 0:full * nq], ps[:, 4 + u % 2, 0:full * nq], ACT.Copy) \
                   .then_inc(probT_ready.sem, 1)

            def outputs(L, u):
                x, tile = out_use(u), out_tile(u - 1)
                act.wait_ge(s_made[x % 2].sem, s_made[x % 2].at(L, x // 2 + 1))
                act.activation(hid_hi[:, tile, :], s_flat(x)[:, 0:TOK], ACT.Copy).then_inc(att_hi.sem, 1)

            def attention(L):
                softmax_exp(L, 0)
                softmax_exp(L, 1)
                act.wait_ge(O_ms.sem, O_ms.at(L, 1))
                for j in range(2):
                    act.activation(halves(tmp[:, 2 + j, :]), ps[:, 4 + 2 * j:6 + 2 * j, 0:HALF], ACT.Sqrt,
                                   bias=eps[:, 0:1]).then_inc(O_root.sem, 1)
                copy_t(L, 0)
                softmax_exp(L, 2)
                for u in range(UNITS):
                    if u + 1 < UNITS:
                        copy_t(L, u + 1)
                    if u and u % PAIR_UNITS == 0:
                        outputs(L, u)
                    if opens_mla_pair(u + 3):
                        project(L, u + 3)
                    if u + 3 < UNITS:
                        softmax_exp(L, u + 3)
                    if u == HEAD_HI:
                        act.wait_ge(O_norm.sem, O_norm.at(L, 4))
                        act.activation(hid_hi[:, 6:8, :], tmp[:, 4:6, :], ACT.Copy).then_inc(O_hi.sem, 1)
                outputs(L, UNITS)

            with act.Fori(0, DEPTH) as L:
                ffn(L, "ffn1")
                mixer_inputs(L)
                hgrn(L)
                attention(L)
                for m in range(KD):
                    step(L, CH[f"out{m}"])
                    act.wait_ge(drained.sem, drained.at(L, US[f"out{m}"] + 1))
                    xg_split(m, PAR["ffn2"])
                act.activation(p_hi[:, :, :], p_raw[:, :, :], ACT.Copy).then_inc(p_split.sem, 1)
                ffn(L, "ffn2")
                for half in range(2):
                    step(L, CH[f"proj{half}"])
                    for m in range(4 * half, 4 * half + 4):
                        step(L, CH[f"gate{m}"])
                        if m == 0:
                            root(L, "ple.norm", 1.0, r[:, :], 0)
                        act.wait_ge(drained.sem, drained.at(L, US[f"gate{m}"] + 1))
                        act.activation(gate[:, m % 2, :], gate[:, m % 2, :], ACT.Sigmoid) \
                           .then_inc(sig_done.sem, 1)
                for t in range(KD):
                    act.wait_ge(h_emb.sem, h_emb.at(L, t + 1))
                    xg_split(t, PAR["next"])
            act.wait_ge(made.sem, DEPTH * N_US + made.seed + 1)
            act.activation(halves(r[:, :]), slot(0), ACT.Sqrt, bias=eps[:, 0:1]).then_inc(root_done.sem, 1)

        @block.vector
        def _(dve):
            dve.memset(eps[:, :], EPS).then_inc(drained.sem, 4)
            dve.memset(no_sink[:, :], 0.0).then_inc(wlo_ready.sem, RAW_SLOTS)
            dve.memset(r_col[:, :], 1.0)
            dve.memset(lb[:, :], 0.0)

            def split_lo(layer, n, more=0):
                s = n % W_SLOTS
                dve.wait_ge(whi_ready.sem, whi_ready.at(layer, n + 1, more * 4))
                dve.tensor_tensor(w_lo[:, s, :], w_raw[:, n % RAW_SLOTS, :], w_hi[:, s, :].bitcast(F32),
                                  ALU.subtract).then_inc(wlo_ready.sem, 1)

            def step(layer, n, more=0):
                split_lo(layer, n + AHEAD, more) if n + AHEAD < N_CH else split_lo(layer + 1, n + AHEAD - N_CH, more)

            def inverse(layer, use, roots, out, early=None):
                dve.wait_ge(root_done.sem, root_done.at(layer, roots))
                if use == "mix.norm":
                    dve.reciprocal(r_col[:, :], r_col[:, :])
                if early is None:
                    dve.reciprocal(out, out).then_inc(drained.sem, 1)
                    dve.wait_ge(drained.sem, drained.at(layer, US[use] + 1))
                else:
                    dve.reciprocal(out, out).then_inc(inverted.sem, 1)
                    dve.wait_ge(inverted.sem, inverted.at(layer, early))

            def scaled(layer, u, out, more=0):
                dve.wait_ge(made.sem, made.at(layer, u + 1, more * 4))
                return dve.tensor_tensor(out, slot(u), halves(r[:, :]), ALU.mult)

            def xg_rest(layer, t, count, gain):
                dve.wait_ge(xhi_ready.sem, count)
                dve.scalar_tensor_tensor(xg_lo[:, t, :], h[:, t, :], par[:, gain + t:gain + t + 1],
                                         xg_hi[:, t, :].bitcast(F32), ALU.mult, ALU.subtract) \
                   .then_inc(xg_ready.sem, 1)

            dve.wait_ge(x_in.sem, 32)
            for t in range(KD):
                xg_rest(0, t, t + 1, PAR["next"])
            for n in range(AHEAD):
                split_lo(0, n)
            dve.wait_ge(const_in.sem, 16 * 9)
            dve.tensor_copy(mask[:, :, :], mask_f[:, :, :])
            dve.tensor_tensor(lbt[:, 0, :], lbl[:, 0, :], lbl[:, 1, :], ALU.max).then_inc(lb_step.sem, 1)
            dve.wait_ge(lb_step.sem, 1)
            dve.tensor_tensor(lbt[:, 1, :], lbl[:, 0, :], lbt[:, 0, :], ALU.subtract).then_inc(lb_step.sem, 1)
            dve.tensor_tensor(lbt[:, 2, :], lbl[:, 1, :], lbt[:, 0, :], ALU.subtract).then_inc(lb_step.sem, 1)
            dve.wait_ge(lb_exp.sem, 1)
            dve.tensor_tensor(lbt[:, 3, :], lbt[:, 1, :], lbt[:, 2, :], ALU.add).then_inc(lb_step.sem, 1)
            dve.wait_ge(lb_step.sem, 4)
            dve.reciprocal(lbt[:, 3, :], lbt[:, 3, :]).then_inc(lb_step.sem, 1)
            dve.wait_ge(lb_step.sem, 5)
            dve.tensor_tensor(lbt[:, 1, :], lbt[:, 1, :], lbt[:, 3, :], ALU.mult).then_inc(lb_step.sem, 1)
            dve.tensor_tensor(lbt[:, 2, :], lbt[:, 2, :], lbt[:, 3, :], ALU.mult).then_inc(lb_step.sem, 1)
            dve.wait_ge(lb_step.sem, 7)
            dve.tensor_tensor(lbt[:, 2, :], lbt[:, 2, :], lbt[:, 1, :], ALU.add).then_inc(lb_step.sem, 1)
            dve.wait_ge(lb_step.sem, 8)
            dve.tensor_tensor(lb_next[:, :], lbt[:, 2, :], lbt[:, 1, :], ALU.subtract).then_inc(lb_step.sem, 1)
            dve.wait_ge(lb_step.sem, 9)

            def ffn(L, f):
                roots = 1 if f == "ffn1" else 6
                for g, pairs in enumerate(FF_GROUPS):
                    c0, u0 = CH[f"{f}.{g}.up0"], US[f"{f}.{g}.up0"]
                    j0 = hid_before(f, g)

                    def two_pairs(i, c, u, tile, first):
                        for pr in range(2):
                            step(L, c + 2 * pr, i)
                            if first and pr == 0:
                                step(L, c + 1, i)
                                inverse(L, f"{f}.norm", roots, r[:, :], 1 if f == "ffn1" else 3)
                            ug = u + 2 * pr + (1 if first and pr else 0)
                            scaled(L, ug, halves(gate[:, pr, :]), i).then_inc(drained.sem, 1)
                            if not (first and pr == 0):
                                step(L, c + 2 * pr + 1, i)
                            scaled(L, ug + 1, halves(val[:, pr, :]), i) \
                                .then_inc(drained.sem, 2 if first and pr == 0 else 1)
                            j = j0 + tile + pr
                            dve.wait_ge(drained.sem, drained.at(L, ug + 2, i * 4))
                            dve.wait_ge(silu_done.sem, silu_done.at(L, j + 1, i * 2))
                            dve.tensor_tensor(val[:, pr, :], gate[:, pr, :], val[:, pr, :], ALU.mult) \
                               .then_inc(prod_done.sem, 1)
                            dve.wait_ge(hidhi_ready.sem, hidhi_ready.at(L, j + 1, i * 2))
                            dve.tensor_tensor(hid_lo[:, tile + pr + i * 2, :], val[:, pr, :],
                                              hid_hi[:, tile + pr + i * 2, :].bitcast(F32), ALU.subtract) \
                               .then_inc(hid_ready.sem, 1)

                    if g == 0:
                        two_pairs(0, c0, u0, 0, True)
                        with dve.Fori(0, pairs // 2 - 1) as i:
                            two_pairs(i, c0 + 4, u0 + 5, 2, False)
                    else:
                        with dve.Fori(0, pairs // 2) as i:
                            two_pairs(i, c0, u0, 0, False)
                    d0, v0 = CH[f"{f}.{g}.down0"], US[f"{f}.{g}.down0"]

                    def down(m, q, i):
                        dve.wait_ge(made.sem, made.at(L, v0 + q + 1, i * 4))
                        dve.scalar_tensor_tensor(halves(h[:, m, :]), slot(v0 + q), 0.5, halves(h[:, m, :]),
                                                 ALU.mult, ALU.add).then_inc(drained.sem, 1)

                    if g < len(FF_GROUPS) - 1:
                        with dve.Fori(0, KD // 4) as i:
                            for q in range(4):
                                step(L, d0 + q, i)
                                down(q + i * 4, q, i)
                        continue
                    gain, before = (PAR["mix"], 0) if f == "ffn1" else (PAR["ple"], 16)
                    for m in range(KD):
                        step(L, d0 + m)
                        down(m, m, 0)
                        if m:
                            xg_rest(L, m - 1, xhi_ready.at(L, before + m), gain)
                    xg_rest(L, KD - 1, xhi_ready.at(L, before + KD), gain)

            def gates(L):
                dve.wait_ge(f_exp.sem, f_exp.at(L, 1))
                dve.tensor_scalar(one_minus_lb[:, :], lb[:, :], -1.0, 1.0, ALU.mult, ALU.add) \
                   .then_inc(f_step.sem, 1)
                dve.tensor_scalar(fx[:, :, :], fx[:, :, :], 1.0, None, ALU.add).then_inc(f_step.sem, 1)
                dve.wait_ge(f_step.sem, f_step.at(L, 2))
                dve.reciprocal(fx[:, :, :], fx[:, :, :]).then_inc(f_step.sem, 1)
                dve.wait_ge(f_step.sem, f_step.at(L, 3))
                for j in range(2):
                    dve.tensor_scalar(fx[:, j, :], fx[:, j, :], one_minus_lb[:, j:j + 1], lb[:, j:j + 1],
                                      ALU.mult, ALU.add).then_inc(f_step.sem, 1)
                dve.wait_ge(f_step.sem, f_step.at(L, 5))
                dve.tensor_scalar(hk[:, :, :], fx[:, :, :], -1.0, 1.0, ALU.mult, ALU.add).then_inc(f_step.sem, 1)
                dve.tensor_scalar(fx[:, :, :], fx[:, :, :], TINY, None, ALU.max).then_inc(f_step.sem, 1)
                dve.tensor_copy(lb[:, :], lb_next[:, :]).then_inc(f_step.sem, 1)

            def decays(L):
                dve.wait_ge(f_ln.sem, f_ln.at(L, 1))
                for j in range(2):
                    for t0, tn in BLOCKS:
                        dve.tensor_tensor_scan(G[:, j, t0:t0 + tn], fx[:, j, t0:t0 + tn], fx[:, j, t0:t0 + tn],
                                               0.0, ALU.add, ALU.bypass).then_inc(G_ready.sem, 1)
                dve.wait_ge(G_ready.sem, G_ready.at(L, 10))
                for j in range(2):
                    g4 = G[:, j, 0:PROMPT].rearrange("p (b t) -> p b t", b=4)
                    dve.tensor_tensor(kd[:, j, 0:PROMPT].rearrange("p (b t) -> p b t", b=4),
                                      g4[:, :, P - 1:P].to_broadcast([P, 4, P]), g4, ALU.subtract) \
                       .then_inc(kd_diff.sem, 1)
                dve.tensor_tensor(kd[:, :, PROMPT:], G[:, :, TOK - 1:TOK].to_broadcast([P, 2, SAMPLE]),
                                  G[:, :, PROMPT:], ALU.subtract).then_inc(kd_diff.sem, 1)

            def decayed(L):
                dve.wait_ge(eG_ready.sem, eG_ready.at(L, 1))
                dve.wait_ge(silu_in.sem, silu_in.at(L, 2))
                dve.tensor_tensor(qG[:, :, :], hq[:, :, :], eG[:, :, :], ALU.mult).then_inc(qG_ready.sem, 1)
                dve.tensor_copy(e_end[:, :, 0:4], eG[:, :, P - 1:PROMPT:P]).then_inc(qG_ready.sem, 1)
                dve.tensor_copy(e_end[:, :, 4:5], eG[:, :, TOK - 1:TOK]).then_inc(qG_ready.sem, 1)
                dve.wait_ge(kd_exp.sem, kd_exp.at(L, 1))
                dve.tensor_tensor(kd[:, :, :], hk[:, :, :], kd[:, :, :], ALU.mult).then_inc(kd_ready.sem, 1)

            def mixer_inputs(L):
                for name in W_IN:
                    step(L, CH[name])
                    if name == "g1":
                        gates(L)
                    if name == "ckv":
                        decays(L)
                    if name == "cq0":
                        decayed(L)
                    if name == "f0" or name == "spare":
                        continue
                    if name == "f1":
                        inverse(L, "mix.norm", 3, r[:, :], 2)
                        for j in range(2):
                            scaled(L, US[f"f{j}"], halves(fx[:, j, :])).then_inc(drained.sem, 1 + j)
                        continue
                    u = US[name]
                    if name[0] in "qg":
                        dst = (hq if name[0] == "q" else hg)[:, int(name[1]), :]
                        scaled(L, u, halves(dst)).then_inc(drained.sem, 1)
                    elif name in ("i0", "i1", "swv"):
                        dve.wait_ge(made.sem, made.at(L, u + 1))
                        for b in range(5):
                            rows = P if b < 4 else 64
                            if name == "swv":
                                dst = swv[0:rows, b if b < 4 else 5, :]
                            else:
                                dst = V[0:rows, b, 128 * int(name[1]):128 * int(name[1]) + 128]
                            src = ps[0:rows, bank(u) + b // 4, 128 * (b % 4):128 * (b % 4) + 128]
                            ins = dve.tensor_scalar(dst, src, r_col[0:rows, b:b + 1], None, ALU.mult)
                        ins.then_inc(drained.sem, 1)
                    elif name == "ckv":
                        scaled(L, u, halves(tmp[:, 0, :])).then_inc(drained.sem, 1)
                    elif name == "kr":
                        scaled(L, u, halves(tmp[:, 2, :])).then_inc(drained.sem, 1)
                        dve.wait_ge(drained.sem, drained.at(L, u + 1))
                        dve.tensor_tensor(tmp[:, 2, :], tmp[:, 2, :], cs[:, :], ALU.mult).then_inc(c_raw.sem, 1)
                    elif name in ("cq0", "cq1"):
                        scaled(L, u, halves(cq[:, int(name[2]), :])).then_inc(drained.sem, 1)
                    elif name == "swk":
                        inverse(L, "ckv.norm", 4, tmp[:, 5, :])
                        for lo, hi, to in ((0, PROMPT, 0), (PROMPT, TOK, PROMPT + PAST)):
                            dve.scalar_tensor_tensor(ckv[:, to:to + hi - lo], tmp[:, 0, lo:hi],
                                                     par[:, PAR["kv_norm"]:PAR["kv_norm"] + 1],
                                                     tmp[:, 5, lo:hi], ALU.mult, ALU.mult).then_inc(c_norm.sem, 1)
                        dve.wait_ge(made.sem, made.at(L, u + 1))
                        flat = ps[:, bank(u):bank(u) + 2, 0:HALF]
                        dve.tensor_tensor(swk[:, 0:HALF], ps[:, bank(u), 0:HALF], r[:, 0:HALF], ALU.mult) \
                           .then_inc(c_norm.sem, 1)
                        dve.tensor_tensor(swk[:, HALF:PROMPT], ps[:, bank(u) + 1, 0:PROMPT - HALF],
                                          r[:, HALF:PROMPT], ALU.mult).then_inc(c_norm.sem, 1)
                        dve.tensor_tensor(swk[:, PROMPT + 128:], ps[:, bank(u) + 1, PROMPT - HALF:HALF],
                                          r[:, PROMPT:], ALU.mult).then_inc(drained.sem, 1)
                        dve.wait_ge(made.sem, made.at(L, US["kr.sum"] + 1))
                        dve.tensor_copy(halves(krs[64:96, :]),
                                        ps[64:96, bank(US["kr.sum"]):bank(US["kr.sum"]) + 2, 0:HALF]) \
                           .then_inc(drained.sem, 1)
                        inverse(L, "cq.norm", 5, tmp[:, 1, :])
                        for j in range(2):
                            dve.scalar_tensor_tensor(cq[:, j, :], cq[:, j, :],
                                                     par[:, PAR["q_norm"] + j:PAR["q_norm"] + j + 1],
                                                     tmp[:, 1, :], ALU.mult, ALU.mult).then_inc(c_norm.sem, 1)
                    else:
                        scaled(L, u, halves(swq[:, int(name[3]), :])).then_inc(drained.sem, 1)
                dve.tensor_scalar(no_sink[:, :], par[:, PAR["sink"]:PAR["sink"] + 6], -1.0, None, ALU.mult) \
                   .then_inc(c_norm.sem, 1)

            def diff(L, n):
                j, lv = divmod(n, LEVELS)
                if lv == 0:
                    return
                m = 1 << lv
                width = PROMPT if m == P else TOK
                g = G[:, j, 0:width].rearrange("p (s t) -> p s t", t=m)
                e = tmp[:, n % 2, 0:width].rearrange("p (s t) -> p s t", t=m)
                mid = g[:, :, m // 2 - 1:m // 2].to_broadcast([P, width // m, m // 2])
                before = n - 2 - (n - 2) // LEVELS
                if before > 0:
                    dve.wait_ge(lv_qk.sem, lv_qk.at(L, 2 * before))
                dve.tensor_tensor(e[:, :, 0:m // 2], mid, g[:, :, 0:m // 2], ALU.subtract) \
                   .then_inc(lv_diff.sem, 1)
                dve.tensor_tensor(e[:, :, m // 2:], g[:, :, m // 2:], mid, ALU.subtract) \
                   .then_inc(lv_diff.sem, 1)

            def hgrn(L):
                diff(L, 1)
                dve.wait_ge(qG_ready.sem, qG_ready.at(L, 3))
                dve.wait_ge(dS_made.sem, dS_made.at(L, 1))
                for b in range(4):
                    for j in range(2):
                        d = ps[:, 4 + j, 64 * b:64 * b + 64]
                        if b == 0:
                            dve.tensor_copy(S[:, j, 1, :], d).then_inc(S_ready.sem, 1)
                            continue
                        dve.wait_ge(S_ready.sem, S_ready.at(L, 2 * b + j - 1))
                        dve.scalar_tensor_tensor(S[:, j, b + 1, :], S[:, j, b, :], e_end[:, j, b:b + 1], d,
                                                 ALU.mult, ALU.add).then_inc(S_ready.sem, 1)
                for j in range(2):
                    dve.scalar_tensor_tensor(S[:, j, 6, :], S[:, j, 5, :], e_end[:, j, 4:5],
                                             ps[:, 4 + j, 256:320], ALU.mult, ALU.add).then_inc(S_ready.sem, 1)

                def products(n):
                    j, lv = divmod(n, LEVELS)
                    if lv == 0:
                        return
                    width = PROMPT if lv == LEVELS - 1 else TOK
                    dve.wait_ge(lv_exp.sem, lv_exp.at(L, n - j))
                    e = tmp[:, n % 2, 0:width]
                    dve.tensor_tensor(tmp[:, 2 + n % 2, 0:width], hq[:, j, 0:width], e, ALU.mult) \
                       .then_inc(lv_qk.sem, 1)
                    dve.tensor_tensor(tmp[:, 4 + n % 2, 0:width], hk[:, j, 0:width], e, ALU.mult) \
                       .then_inc(lv_qk.sem, 1)

                def take(n):
                    j, lv = divmod(n, LEVELS)
                    big = ps[:, 3 * (n % 2):3 * (n % 2) + 2, :].rearrange("p a (b t) -> p (a b) t", b=4)
                    small = ps[0:64, 3 * (n % 2) + 2, 0:128].rearrange("p (a t) -> p a t", a=2)
                    dve.wait_ge(A_made.sem, A_made.at(L, n + 1))
                    a8 = A[:, :, :, :].rearrange("p a b t -> p (a b) t")
                    if lv == 0:
                        if j:
                            dve.wait_ge(O_made.sem, O_made.at(L, 1))
                        dve.tensor_tensor(a8, big, ident[:, :].unsqueeze(1).to_broadcast([P, 8, P]), ALU.mult) \
                           .then_inc(A_taken.sem, 1)
                        dve.tensor_tensor(a_tail[:, :, :], small,
                                          ident[0:64, 0:64].unsqueeze(1).to_broadcast([64, 2, 64]), ALU.mult) \
                           .then_inc(A_taken.sem, 1)
                        return
                    dve.wait_ge(A_taken.sem, A_taken.at(L, 2 * n))
                    by_itself(dve)
                    mk = mask[:, lv - 1, :]
                    ins = dve.copy_predicated(a8, mk.unsqueeze(1).to_broadcast([P, 8, P]), big)
                    if lv == LEVELS - 1:
                        ins.then_inc(A_taken.sem, 2)
                        return
                    ins.then_inc(A_taken.sem, 1)
                    dve.copy_predicated(a_tail[:, :, :],
                                        mask[0:64, lv - 1, 0:64].unsqueeze(1).to_broadcast([64, 2, 64]), small) \
                       .then_inc(A_taken.sem, 1)

                n_steps = 2 * LEVELS
                for n in range(n_steps + 1):
                    if 0 < n and n + 1 < n_steps:
                        diff(L, n + 1)
                    if n < n_steps:
                        products(n)
                    if n:
                        take(n - 1)

            def head_norm(L, u):
                part = u / 2
                flat = lambda t: t.rearrange("p a n -> p (a n)")
                if part in (0, 1):
                    dve.wait_ge(O_root.sem, O_root.at(L, u // 2 + 1))
                    dve.reciprocal(tmp[:, 2 + u // 2, :], tmp[:, 2 + u // 2, :]).then_inc(O_norm.sem, 1)
                if part == 2:
                    dve.wait_ge(O_norm.sem, O_norm.at(L, 2))
                    dve.scalar_tensor_tensor(flat(tmp[:, 4:6, :]), flat(hk[:, :, :]),
                                             par[:, PAR["hg_out"]:PAR["hg_out"] + 1], flat(tmp[:, 2:4, :]),
                                             ALU.mult, ALU.mult).then_inc(O_norm.sem, 1)
                if part == 3:
                    dve.wait_ge(O_norm.sem, O_norm.at(L, 3))
                    dve.tensor_tensor(tmp[:, 4:6, :], tmp[:, 4:6, :], hg[:, :, :], ALU.mult) \
                       .then_inc(O_norm.sem, 1)
                if u == HEAD_HI + 1:
                    dve.wait_ge(O_hi.sem, O_hi.at(L, 1))
                    dve.tensor_tensor(hid_lo[:, 6:8, :], tmp[:, 4:6, :], hid_hi[:, 6:8, :].bitcast(F32),
                                      ALU.subtract).then_inc(O_lo.sem, 1)

            def project(L, u):
                x = unit(u)[3] - PROJECTIONS + 1
                dve.wait_ge(s_made[x % 2].sem, s_made[x % 2].at(L, x // 2 + 1))
                dve.tensor_tensor(halves(tq[:, :]), ps[:, 2 * (x % 2):2 * (x % 2) + 2, 0:HALF],
                                  halves(cs[:, :]), ALU.mult).then_inc(s_free[x % 2].sem, 1)
                for a in range(2):
                    x += 2
                    dve.wait_ge(s_made[x % 2].sem, s_made[x % 2].at(L, x // 2 + 1))
                    dve.tensor_copy(halves(qT[a][0:96, :]), ps[0:96, 2 * (x % 2):2 * (x % 2) + 2, 0:HALF]) \
                       .then_inc(s_free[x % 2].sem, 1)

            def bound(L, u):
                kind, pr, v, x = unit(u)
                b = u % 2
                nq, nk = UNIT_Q[v % 5], unit_keys(kind, v % 5)
                src = ps[:, 2 * (x % 2):2 * (x % 2) + 2, :].rearrange("p a n -> p (a n)")[0:nq, 0:nk]
                dve.wait_ge(s_made[x % 2].sem, s_made[x % 2].at(L, x // 2 + 1))
                if kind == "swa":
                    hd = pr + 3 * (v // 5)
                    slope = 2.0 ** (-8.0 * (hd + 1) / 6)
                    k0 = 128 if v % 5 == 0 else 0
                    dve.scalar_tensor_tensor(score[0:nq, b, 0:nk], dist[0:nq, k0:k0 + nk], -slope / SWA_SCALE,
                                             src, ALU.mult, ALU.add).then_inc(scored.sem, 1)
                    dve.wait_ge(scored.sem, scored.at(L, u + 1))
                    dve.reduce_max(stat[0:nq, b, 0:1], score[0:nq, b, 0:nk], AX.X) \
                       .then_inc(s_free[x % 2].sem, 1)
                    dve.wait_ge(s_free[x % 2].sem, s_free[x % 2].at(L, x // 2 + 1))
                    dve.tensor_scalar(stat[0:nq, b, 1:2], stat[0:nq, b, 0:1], -SWA_SCALE,
                                      no_sink[0:nq, hd:hd + 1], ALU.mult, ALU.min).then_inc(bound_done.sem, 1)
                    return
                dve.reduce_max(stat[0:nq, b, 0:1], src, AX.X).then_inc(scored.sem, 1)
                dve.wait_ge(scored.sem, scored.at(L, u + 1))
                dve.tensor_scalar(stat[0:nq, b, 1:2], stat[0:nq, b, 0:1], -MLA_SCALE, None,
                                  ALU.mult).then_inc(bound_done.sem, 1)

            def invert(L, u):
                kind, _, v, x = unit(u)
                b = u % 2
                nq, nk = UNIT_Q[v % 5], unit_keys(kind, v % 5)
                exp_wait(dve, L, u)
                if u >= 2:
                    dve.wait_ge(o_taken.sem, o_taken.at(L, u - 1))
                if kind == "mla":
                    dve.reciprocal(stat[0:nq, b, 4:5], stat[0:nq, b, 2:3]).then_inc(recip_done.sem, 1)
                else:
                    dve.wait_ge(sink_done.sem, sink_done.at(L, u + 1))
                    dve.tensor_tensor(stat[0:nq, b, 3:4], stat[0:nq, b, 2:3], stat[0:nq, b, 3:4],
                                      ALU.add).then_inc(den_done.sem, 1)
                    dve.wait_ge(den_done.sem, den_done.at(L, u + 1))
                    dve.reciprocal(stat[0:nq, b, 4:5], stat[0:nq, b, 3:4]).then_inc(recip_done.sem, 1)

            def take_out(L, u):
                kind, _, v, x = unit(u)
                a, b = divmod(v, 5)
                nq = UNIT_Q[b]
                dve.wait_ge(pv_done.sem, pv_done.at(L, u + 1))
                dve.wait_ge(recip_done.sem, recip_done.at(L, u + 1))
                dve.tensor_scalar(o_tok[0:nq, (u // PAIR_UNITS) % 2, b, 64 * a:64 * a + 64],
                                  ps[0:nq, 6 + u % 2, 0:64],
                                  stat[0:nq, u % 2, 4:5], None, ALU.mult).then_inc(o_taken.sem, 1)

            def outputs(L, u):
                x, tile, n = out_use(u), out_tile(u - 1), u // PAIR_UNITS
                dve.wait_ge(att_hi.sem, att_hi.at(L, n))
                dve.tensor_tensor(hid_lo[:, tile, :],
                                  ps[:, 2 * (x % 2):2 * (x % 2) + 2, :].rearrange("p a n -> p (a n)")[:, 0:TOK],
                                  hid_hi[:, tile, :].bitcast(F32), ALU.subtract).then_inc(s_free[x % 2].sem, 1)

            def attention(L):
                bound(L, 0)
                bound(L, 1)
                invert(L, 0)
                bound(L, 2)
                for u in range(UNITS):
                    if u + 1 < UNITS:
                        invert(L, u + 1)
                    if u and u % PAIR_UNITS == 0:
                        outputs(L, u)
                    if opens_mla_pair(u + 3):
                        project(L, u + 3)
                    if u + 3 < UNITS:
                        bound(L, u + 3)
                    head_norm(L, u)
                    take_out(L, u)
                outputs(L, UNITS)

            with dve.Fori(0, DEPTH) as L:
                ffn(L, "ffn1")
                mixer_inputs(L)
                hgrn(L)
                attention(L)
                for m in range(KD):
                    step(L, CH[f"out{m}"])
                    u = US[f"out{m}"]
                    dve.wait_ge(made.sem, made.at(L, u + 1))
                    dve.tensor_tensor(halves(h[:, m, :]), slot(u), halves(h[:, m, :]), ALU.add) \
                       .then_inc(drained.sem, 1)
                    if m:
                        xg_rest(L, m - 1, xhi_ready.at(L, 8 + m), PAR["ffn2"])
                xg_rest(L, KD - 1, xhi_ready.at(L, 16), PAR["ffn2"])
                dve.wait_ge(p_split.sem, p_split.at(L, 1))
                dve.tensor_tensor(p_lo[:, :, :], p_raw[:, :, :], p_hi[:, :, :].bitcast(F32), ALU.subtract) \
                   .then_inc(p_ready.sem, 1)
                ffn(L, "ffn2")
                for half in range(2):
                    step(L, CH[f"proj{half}"])
                    for m in range(4):
                        u = US[f"proj{half}.{m}"]
                        dve.wait_ge(made.sem, made.at(L, u + 1))
                        dve.tensor_copy(halves(pp[:, m, :]), slot(u)).then_inc(drained.sem, 1)
                    for m in range(4 * half, 4 * half + 4):
                        step(L, CH[f"gate{m}"])
                        u = US[f"gate{m}"]
                        if m == 0:
                            inverse(L, "ple.norm", 7, r[:, :], 4)
                        last = 1 if m == 0 else PAD_US if m == KD - 1 else 0
                        scaled(L, u, halves(gate[:, m % 2, :])).then_inc(drained.sem, 1 + last)
                        dve.wait_ge(sig_done.sem, sig_done.at(L, m + 1))
                        dve.tensor_tensor(val[:, m % 2, :], gate[:, m % 2, :], pp[:, m % 4, :], ALU.mult) \
                           .then_inc(emb_mul.sem, 1)
                        dve.wait_ge(emb_mul.sem, emb_mul.at(L, m + 1))
                        dve.tensor_tensor(h[:, m, :], h[:, m, :], val[:, m % 2, :], ALU.add) \
                           .then_inc(h_emb.sem, 1)
                for t in range(KD):
                    xg_rest(L, t, xhi_ready.at(L, 24 + t + 1), PAR["next"])
            dve.wait_ge(root_done.sem, DEPTH * root_done.per + 1)
            dve.reciprocal(r[:, :], r[:, :]).then_inc(lb_step.sem, 1)
            dve.wait_ge(lb_step.sem, 10)
            for t in range(KD):
                dve.scalar_tensor_tensor(y[:, t, :], h[:, t, :], par[:, PAR["next"] + t:PAR["next"] + t + 1],
                                         r[:, :], ALU.mult, ALU.mult).then_inc(y_done.sem, 1)

        @block.gpsimd
        def _(pool):
            def square(t, sq_count, acc_count):
                if t == 0:
                    pool.tensor_tensor(acc[:, :], h[:, 0, :], h[:, 0, :], ALU.mult).then_inc(acc_done.sem, 1)
                    return
                pool.wait_ge(acc_done.sem, acc_count)
                pool.tensor_tensor(sq[:, :], h[:, t, :], h[:, t, :], ALU.mult).then_inc(sq_done.sem, 1)
                pool.wait_ge(sq_done.sem, sq_count)
                pool.tensor_tensor(acc[:, :], acc[:, :], sq[:, :], ALU.add).then_inc(acc_done.sem, 1)

            def squares(L, set_no, wait, norm):
                for t in range(KD):
                    wait(t)
                    if t == 0:
                        pool.wait_ge(made.sem, made.at(L, US[norm] + 1))
                    square(t, sq_done.at(L, 7 * set_no + t), acc_done.at(L, 8 * set_no + t))

            pool.wait_ge(x_in.sem, 32)
            for t in range(KD):
                square(t, t, t)

            with pool.Fori(0, DEPTH) as L:
                squares(L, 0, lambda t: pool.wait_ge(drained.sem, drained.at(L, US[f"ffn1.2.down{t}"] + 1)),
                        "ffn1.norm")
                pool.wait_ge(drained.sem, drained.at(L, US["ckv"] + 1))
                pool.tensor_tensor(tmp[:, 1, :], tmp[:, 0, :], tmp[:, 0, :], ALU.mult).then_inc(c_sq.sem, 1)
                for j in range(2):
                    pool.wait_ge(drained.sem, drained.at(L, US[f"cq{j}"] + 1))
                    pool.tensor_tensor(tmp[:, 3 + j, :], cq[:, j, :], cq[:, j, :], ALU.mult).then_inc(c_sq.sem, 1)
                pool.wait_ge(drained.sem, drained.at(L, US["swq2"] + 1))
                by_itself(pool)
                for a in range(2):
                    pool.tensor_copy(kT[a][64:96, 0:PROMPT], krs[64:96, 0:PROMPT]).then_inc(k_placed.sem, 1)
                    pool.tensor_copy(kT[a][64:96, PROMPT + PAST:], krs[64:96, PROMPT:]).then_inc(k_placed.sem, 1)
                squares(L, 1, lambda t: pool.wait_ge(drained.sem, drained.at(L, US[f"out{t}"] + 1)), "mix.norm")
                squares(L, 2, lambda t: pool.wait_ge(drained.sem, drained.at(L, US[f"ffn2.2.down{t}"] + 1)),
                        "ffn2.norm")
                squares(L, 3, lambda t: pool.wait_ge(h_emb.sem, h_emb.at(L, t + 1)), "ple.norm")

        @block.tensor
        def _(pe):
            pe.sem_inc(made.sem, made.seed)
            for parity in range(2):
                pe.sem_inc(s_free[parity].sem, 1)

            def ready(layer, n, u, more=0):
                pe.wait_ge(wlo_ready.sem, wlo_ready.at(layer, n + 1, more * 4))
                pe.wait_ge(drained.sem, layer * N_US + (u + 1) + more * 4)

            def dense(n, u, src_hi, src_lo, kts, w_at=lambda k: k * P, wait=None):
                s = n % W_SLOTS
                for k in kts:
                    if wait is not None:
                        wait(k)
                    wh, wl = (w[:, s, w_at(k):w_at(k) + P] for w in (w_hi, w_lo))
                    for i, (w, m) in enumerate(((wh, src_hi), (wh, src_lo), (wl, src_hi))):
                        for c in range(2):
                            ins = pe.matmul(ps[:, bank(u) + c, 0:HALF], w, m[:, k, c * HALF:(c + 1) * HALF],
                                            start=(k == kts[0] and i == 0), stop=(k == kts[-1] and i == 2))
                return ins

            def norm(layer, use, acc_count, columns=False):
                u = US[use]
                pe.wait_ge(drained.sem, layer * N_US + (u + 1))
                pe.wait_ge(acc_done.sem, acc_count)
                if columns:
                    for b, (t0, tn) in enumerate(BLOCKS):
                        pe.matmul(ps[0:tn, bank(u), 400 + b:401 + b], acc[:, t0:t0 + tn], ones[:, 0:1],
                                  start=True, stop=True)
                for c in range(2):
                    ins = pe.matmul(ps[:, bank(u) + c, 0:HALF], ones[:, :], acc[:, c * HALF:(c + 1) * HALF],
                                    start=True, stop=True)
                ins.then_inc(made.sem, 1)

            KT = tuple(range(KD))

            def xg_wait(count):
                return lambda k: pe.wait_ge(xg_ready.sem, count + k)

            def ffn(L, f):
                set_no = 0 if f == "ffn1" else 2
                for g, pairs in enumerate(FF_GROUPS):
                    c0, u0 = CH[f"{f}.{g}.up0"], US[f"{f}.{g}.up0"]

                    def four(i, c, u, first):
                        for q in range(4):
                            uq_ = u + q + (1 if first and q > 1 else 0)
                            ready(L, c + q, uq_, i)
                            wait = xg_wait(L * 32 + (8 * set_no + 1)) if first and q == 0 else None
                            dense(c + q, uq_, xg_hi, xg_lo, KT, wait=wait).then_inc(made.sem, 1)
                            if first and q == 1:
                                norm(L, f"{f}.norm", L * 32 + 8 * (set_no + 1))

                    if g == 0:
                        four(0, c0, u0, True)
                        with pe.Fori(0, pairs // 2 - 1) as i:
                            four(i, c0 + 4, u0 + 5, False)
                    else:
                        with pe.Fori(0, pairs // 2) as i:
                            four(i, c0, u0, False)
                    d0, v0 = CH[f"{f}.{g}.down0"], US[f"{f}.{g}.down0"]
                    j0 = hid_before(f, g)
                    with pe.Fori(0, KD // 4) as i:
                        for q in range(4):
                            ready(L, d0 + q, v0 + q, i)
                            wait = (lambda k: pe.wait_ge(hid_ready.sem, hid_ready.at(L, j0 + k + 1))) \
                                if q == 0 else None
                            dense(d0 + q, v0 + q, hid_hi, hid_lo, tuple(range(pairs)), wait=wait) \
                                .then_inc(made.sem, 1)

            def mixer_inputs(L):
                for name in W_IN:
                    n = CH[name]
                    if name == "spare":
                        pe.wait_ge(wlo_ready.sem, wlo_ready.at(L, n + 1))
                        continue
                    u = US[name]
                    ready(L, n, u)
                    if name in ("i0", "i1", "swv"):
                        s = n % W_SLOTS
                        for b, (t0, tn) in enumerate(BLOCKS):
                            out = ps[0:tn, bank(u) + b // 4, 128 * (b % 4):128 * (b % 4) + 128]
                            for k in KT:
                                for i, (a, w) in enumerate(((xg_hi, w_hi), (xg_hi, w_lo), (xg_lo, w_hi))):
                                    ins = pe.matmul(out, a[:, k, t0:t0 + tn], w[:, s, k * P:(k + 1) * P],
                                                    start=(k == 0 and i == 0), stop=(k == KD - 1 and i == 2))
                        ins.then_inc(made.sem, 1)
                    else:
                        wait = xg_wait(L * 32 + 9) if name == "f0" else None
                        dense(n, u, xg_hi, xg_lo, KT, wait=wait).then_inc(made.sem, 1)
                    if name == "f1":
                        norm(L, "mix.norm", L * 32 + 16, columns=True)
                    if name == "cq1":
                        small_sum(L, "ckv.norm", [tmp[:, 1, :]], ones[:, :], c_sq.at(L, 1))
                    if name == "swk":
                        u = US["kr.sum"]
                        pe.wait_ge(drained.sem, L * N_US + (u + 1))
                        pe.wait_ge(c_raw.sem, c_raw.at(L, 1))
                        for c in range(2):
                            ins = pe.matmul(ps[0:96, bank(u) + c, 0:HALF], comb[0:64, 0, :],
                                            tmp[0:64, 2, c * HALF:(c + 1) * HALF], start=True, stop=True)
                        ins.then_inc(made.sem, 1)
                        small_sum(L, "cq.norm", [tmp[:, 3, :], tmp[:, 4, :]], ones[:, :], c_sq.at(L, 3))

            def small_sum(L, use, srcs, lhs, count):
                u = US[use]
                pe.wait_ge(drained.sem, L * N_US + (u + 1))
                pe.wait_ge(c_sq.sem, count)
                for i, src in enumerate(srcs):
                    for c in range(2):
                        ins = pe.matmul(ps[:, bank(u) + c, 0:HALF], lhs, src[:, c * HALF:(c + 1) * HALF],
                                        start=(i == 0), stop=(i == len(srcs) - 1))
                ins.then_inc(made.sem, 1)

            def hgrn(L):
                pe.wait_ge(drained.sem, drained.at(L, US["swq2"] + 1))
                pe.wait_ge(kd_ready.sem, kd_ready.at(L, 1))
                for j in range(2):
                    for b, (t0, tn) in enumerate(BLOCKS):
                        ins = pe.transpose(ps[0:tn, 2 * j + b // 4, 128 * (b % 4):128 * (b % 4) + 128],
                                           kd[:, j, t0:t0 + tn], ident[:, :])
                ins.then_inc(kd_turned.sem, 1)
                pe.wait_ge(kdT_ready.sem, kdT_ready.at(L, 4))
                for j in range(2):
                    for a in range(2):
                        for b, (t0, tn) in enumerate(BLOCKS):
                            ins = pe.matmul(ps[64 * a:64 * a + 64, 4 + j, 64 * b:64 * b + 64],
                                            kdT[0:tn, j, b, 64 * a:64 * a + 64],
                                            V[0:tn, b, 128 * j + 64 * a:128 * j + 64 * a + 64],
                                            start=True, stop=True)
                ins.then_inc(dS_made.sem, 1)
                for n in range(2 * LEVELS):
                    j, lv = divmod(n, LEVELS)
                    if lv:
                        pe.wait_ge(lv_qk.sem, lv_qk.at(L, 2 * (n - j)))
                        q, k = tmp[:, 2 + n % 2, :], tmp[:, 4 + n % 2, :]
                    else:
                        q, k = hq[:, j, :], hk[:, j, :]
                    if n == 1:
                        pe.wait_ge(S_ready.sem, S_ready.at(L, 10))
                    if n >= 2:
                        pe.wait_ge(A_taken.sem, A_taken.at(L, 2 * (n - 1)))
                    by_itself(pe)
                    blocks = BLOCKS[:4] if lv == LEVELS - 1 else BLOCKS
                    for a in range(2):
                        rows = slice(64 * a, 64 * a + 64)
                        order = sorted(range(len(blocks)), key=lambda b: (a == 0 and b < 4, b))
                        if a and len(blocks) == 5:
                            pe.wait_ge(tail_made.sem, tail_made.at(L, n - j + 1))
                        for b in order:
                            t0, tn = blocks[b]
                            if b < 4:
                                out = ps[:, 3 * (n % 2) + a, 128 * b:128 * b + 128]
                            else:
                                out = ps[0:64, 3 * (n % 2) + 2, 64 * a:64 * a + 64]
                            ins = pe.matmul(out, k[rows, t0:t0 + tn], q[rows, t0:t0 + tn], start=True, stop=True)
                            if b == 4 and a == 0:
                                ins.then_inc(tail_made.sem, 1)
                    ins.then_inc(A_made.sem, 1)
                    if n == LEVELS:
                        heads(L, 0)
                heads(L, 1)

            def mean_squares(L):
                pe.wait_ge(O_sq.sem, O_sq.at(L, 1))
                for j in range(2):
                    for c in range(2):
                        ins = pe.matmul(ps[:, 4 + 2 * j + c, 0:HALF], head_ones[:, :],
                                        tmp[:, j, c * HALF:(c + 1) * HALF], start=True, stop=True)
                ins.then_inc(O_ms.sem, 1)

            def heads(L, j):
                pe.wait_ge(A_taken.sem, A_taken.at(L, 16 * (j + 1)))
                if j:
                    pe.wait_ge(O_out.sem, O_out.at(L, 2))
                for a in range(2):
                    rows = slice(64 * a, 64 * a + 64)
                    for b, (t0, tn) in enumerate(BLOCKS):
                        out = ps[rows, 6, t0:t0 + tn] if b < 4 else ps[rows, 7, 0:SAMPLE]
                        scores = A[:, a, b, :] if b < 4 else a_tail[:, a, :]
                        ins = pe.matmul(out, V[0:tn, b, 128 * j + 64 * a:128 * j + 64 * a + 64], scores,
                                        start=True, stop=(b == 0))
                        if a and b == 4:
                            ins.then_inc(tail_out.sem, 1)
                            pe.wait_ge(tail_out.sem, tail_out.at(L, j + 1))
                            by_itself(pe)
                        if b:
                            ins = pe.matmul(out, S[rows, j, b if b < 4 else 5, :], qG[rows, j, t0:t0 + tn],
                                            start=False, stop=True)
                ins.then_inc(O_made.sem, 1)

            def take_slot(L, x):
                pe.wait_ge(s_free[x % 2].sem, L * s_free[x % 2].per + (x // 2 + 1))
                return 2 * (x % 2)

            def project(L, u):
                pr, x = unit(u)[1], unit(u)[3] - PROJECTIONS
                if pr == 0:
                    pe.wait_ge(k_placed.sem, k_placed.at(L, 4))
                    pe.wait_ge(late_in.sem, late_in.at(L, late_in.per))
                wk, wv = ukv_w[:, pr, 0:P], ukv_w[:, pr, P:2 * P]
                rot = x + 1

                def query(x, a):
                    b0 = take_slot(L, x)
                    if a == 0:
                        pe.wait_ge(s_free[rot % 2].sem, s_free[rot % 2].at(L, rot // 2 + 1))
                    for c in range(2):
                        pe.matmul(ps[0:96, b0 + c, 0:HALF], comb[:, 1 + a, :], tq[:, c * HALF:(c + 1) * HALF],
                                  start=True, stop=False, skip_group_check=True)
                    for k in range(2):
                        for c in range(2):
                            ins = pe.matmul(ps[0:64, b0 + c, 0:HALF], uq_w[:, k, pr, P + 64 * a:P + 64 * a + 64],
                                            cq[:, k, c * HALF:(c + 1) * HALF], start=False, stop=(k == 1),
                                            skip_group_check=True)
                    ins.then_inc(s_made[x % 2].sem, 1)

                b0 = take_slot(L, x)
                for c in range(2):
                    ins = pe.matmul(ps[:, b0 + c, :], wk, ckv[:, 512 * c:512 * c + 512], start=True, stop=True)
                ins.then_inc(s_made[x % 2].sem, 1)
                b0 = take_slot(L, rot)
                for k in range(2):
                    for c in range(2):
                        ins = pe.matmul(ps[:, b0 + c, 0:HALF], uq_w[:, k, pr, 0:P],
                                        cq[:, k, c * HALF:(c + 1) * HALF], start=(k == 0), stop=(k == 1))
                ins.then_inc(s_made[rot % 2].sem, 1)
                x += 2
                b0 = take_slot(L, x)
                pe.matmul(ps[:, b0, 0:64], wk, ckv[:, 1024:], start=True, stop=True)
                pe.matmul(ps[0:64, b0 + 1, 0:P], ckv[:, 1024:], wv, start=True, stop=True) \
                    .then_inc(s_made[x % 2].sem, 1)
                query(x + 1, 0)
                x += 2
                b0 = take_slot(L, x)
                for t in range(8):
                    ins = pe.matmul(ps[:, b0 + t // 4, 128 * (t % 4):128 * (t % 4) + 128],
                                    ckv[:, 128 * t:128 * t + 128], wv, start=True, stop=True)
                ins.then_inc(s_made[x % 2].sem, 1)
                x += 1
                query(x, 1)
                for back in (0, 1):
                    pe.wait_ge(s_free[(x - back) % 2].sem, s_free[(x - back) % 2].at(L, (x - back) // 2 + 1))

            def scores(L, u):
                kind, pr, v, x = unit(u)
                a, b = divmod(v, 5)
                t0, nq = BLOCKS[b]
                b0 = take_slot(L, x)
                if b == 4 and kind == "swa":
                    by_itself(pe)
                out = ps[:, b0:b0 + 2, :].rearrange("p a n -> p (a n)")
                if kind == "swa":
                    rows = slice(64 * a, 64 * a + 64)
                    q, keys = swq[rows, pr, t0:t0 + nq], swk
                    k0 = (0, 0, 128, 256, 512)[b]
                else:
                    rows = slice(0, 96)
                    q, keys = qT[a][rows, t0:t0 + nq], kT[a]
                    k0 = 0 if b < 4 else PROMPT
                nk = unit_keys(kind, b)
                late_mask = kind == "mla" and b < 4
                if nk > 512:
                    pe.matmul(out[0:nq, 0:512], q, keys[rows, k0:k0 + 512], start=True, stop=True)
                    ins = pe.matmul(out[0:nq, 512:nk], q, keys[rows, k0 + 512:k0 + nk], start=True, stop=True)
                else:
                    ins = pe.matmul(out[0:nq, 0:nk], q, keys[rows, k0:k0 + nk], start=True,
                                    stop=not late_mask, skip_group_check=late_mask)
                if late_mask:
                    ins = pe.matmul(out[:, nk - 64:nk], late[0:1, 0:P], late[0:1, P:P + 64],
                                    start=False, stop=True, skip_group_check=True)
                ins.then_inc(s_made[x % 2].sem, 1)

            def turn(L, u):
                kind, _, v, _ = unit(u)
                b = v % 5
                nq, tiles = UNIT_Q[b], unit_tiles(kind, b)
                exp_wait(pe, L, u)
                if u >= 2:
                    pe.wait_ge(probT_ready.sem, probT_ready.at(L, u - 1))
                if b == 4:
                    by_itself(pe)
                for i in range(len(tiles)):
                    kn = 64 if b == 4 and i == len(tiles) - 1 else P
                    ins = pe.transpose(ps[0:kn, 4 + u % 2, i * nq:(i + 1) * nq],
                                       prob[0:nq, u % 2, 128 * i:128 * i + kn], ident[0:nq, 0:nq])
                ins.then_inc(turned.sem, 1)

            def weigh(L, u):
                kind, pr, v, _ = unit(u)
                a, b = divmod(v, 5)
                t0, nq = BLOCKS[b]
                pe.wait_ge(probT_ready.sem, probT_ready.at(L, u + 1))
                if u >= 2:
                    pe.wait_ge(o_taken.sem, o_taken.at(L, u - 1))
                out = ps[0:nq, 6 + u % 2, 0:64]
                tiles = unit_tiles(kind, b)
                for i, t in enumerate(tiles):
                    kn = 64 if b == 4 and i == len(tiles) - 1 else P
                    values = (swv if kind == "swa" else mv[pr % 2])[0:kn, t, 64 * a:64 * a + 64]
                    ins = pe.matmul(out, probT[0:kn, u % 2, i * nq:(i + 1) * nq], values,
                                    start=(i == 0), stop=(i == len(tiles) - 1))
                ins.then_inc(pv_done.sem, 1)

            def outputs(L, u):
                x = out_use(u)
                b0 = take_slot(L, x)
                pe.wait_ge(o_taken.sem, o_taken.at(L, u))
                for b, (t0, tn) in enumerate(BLOCKS):
                    ins = pe.transpose(ps[:, b0 + b // 4, P * (b % 4):P * (b % 4) + tn],
                                       o_tok[0:tn, (u // PAIR_UNITS - 1) % 2, b, :], ident[0:tn, 0:tn])
                ins.then_inc(s_made[x % 2].sem, 1)

            def attention(L):
                scores(L, 0)
                scores(L, 1)
                mean_squares(L)
                pe.wait_ge(O_root.sem, O_root.at(L, 2))
                by_itself(pe)
                turn(L, 0)
                scores(L, 2)
                for u in range(UNITS):
                    if u + 1 < UNITS:
                        turn(L, u + 1)
                    if u and u % PAIR_UNITS == 0:
                        outputs(L, u)
                    if opens_mla_pair(u + 3):
                        project(L, u + 3)
                    if u + 3 < UNITS:
                        scores(L, u + 3)
                    weigh(L, u)
                outputs(L, UNITS)

            pe.wait_ge(const_in.sem, 16 * 9)
            with pe.Fori(0, DEPTH) as L:
                ffn(L, "ffn1")
                mixer_inputs(L)
                hgrn(L)
                attention(L)
                last = out_use(UNITS)
                mixed = (6, 7, 3, 4, 5, 0, 1, out_tile(UNITS - 1))
                assert sorted(mixed) == list(KT) and US["out0"] % 4 != last % 2

                def split(k):
                    if k == mixed[0]:
                        pe.wait_ge(O_lo.sem, O_lo.at(L, 1))
                    if k == mixed[-1]:
                        pe.wait_ge(s_free[last % 2].sem, s_free[last % 2].at(L, last // 2 + 1))

                for m in range(KD):
                    ready(L, CH[f"out{m}"], US[f"out{m}"])
                    dense(CH[f"out{m}"], US[f"out{m}"], hid_hi, hid_lo, mixed,
                          wait=split if m == 0 else None).then_inc(made.sem, 1)
                ffn(L, "ffn2")
                pe.wait_ge(p_ready.sem, p_ready.at(L, 1))
                for half in range(2):
                    n = CH[f"proj{half}"]
                    for m in range(4):
                        u = US[f"proj{half}.{m}"]
                        ready(L, n, u)
                        dense(n, u, p_hi, p_lo, (0, 1), lambda k, m=m: (2 * m + k) * P).then_inc(made.sem, 1)
                    for m in range(4 * half, 4 * half + 4):
                        u = US[f"gate{m}"]
                        ready(L, CH[f"gate{m}"], u)
                        last = PAD_US if m == KD - 1 else 0
                        dense(CH[f"gate{m}"], u, xg_hi, xg_lo, KT,
                              wait=xg_wait(L * 32 + 25) if m == 0 else None).then_inc(made.sem, 1 + last)
                        if m == 0:
                            norm(L, "ple.norm", L * 32 + 32)
            pe.wait_ge(acc_done.sem, DEPTH * 32 + 8)
            pe.wait_ge(drained.sem, DEPTH * N_US + 1)
            for c in range(2):
                ins = pe.matmul(ps[:, c, 0:HALF], ones[:, :], acc[:, c * HALF:(c + 1) * HALF],
                                start=True, stop=True)
            ins.then_inc(made.sem, 1)


def _chunk(w):
    return w.reshape(-1, P, w.shape[1]).transpose(1, 0, 2).reshape(P, -1)


def _weights(a):
    out = np.zeros((DEPTH * N_CH + AHEAD, P, CHUNK_W), np.float32)
    for i in range(DEPTH):
        def put(name, block):
            out[i * N_CH + CH[name], :, :block.shape[1]] = block

        for f in ("ffn1", "ffn2"):
            up, down = a[f + "_up"][i], a[f + "_down"][i]
            j = 0
            for g, pairs in enumerate(FF_GROUPS):
                for q in range(pairs):
                    put(f"{f}.{g}.up{2 * q}", _chunk(up[:, P * (j + q):P * (j + q + 1)]))
                    put(f"{f}.{g}.up{2 * q + 1}", _chunk(up[:, D_FF + P * (j + q):D_FF + P * (j + q + 1)]))
                for m in range(KD):
                    put(f"{f}.{g}.down{m}", _chunk(down[P * j:P * (j + pairs), P * m:P * (m + 1)]))
                j += pairs
        w = a["w_in"][i]
        mla, swa, hgr = 0, 416, 1056
        kr = w[:, mla + 384:mla + 416]
        swapped = np.concatenate([kr[:, 16:], kr[:, :16]], axis=1)
        cols = {"ckv": w[:, 256:384], "kr": np.concatenate([kr, swapped, kr, swapped], axis=1),
                "swk": w[:, swa + 384:swa + 512], "swv": w[:, swa + 512:swa + 640]}
        for j in range(2):
            cols[f"cq{j}"] = w[:, P * j:P * (j + 1)]
            for s, name in enumerate("qfig"):
                cols[f"{name}{j}"] = w[:, hgr + 256 * s + P * j:hgr + 256 * s + P * (j + 1)]
        for j in range(3):
            cols[f"swq{j}"] = np.concatenate([w[:, swa + 64 * hd:swa + 64 * hd + 64] for hd in (j, j + 3)], axis=1)
        for name, c in cols.items():
            put(name, _chunk(c))
        order = list(range(384))
        for j in range(3):
            for hd in (j, j + 3):
                order += list(range(384 + 64 * hd, 384 + 64 * hd + 64))
        order += list(range(768, 1024))
        wo = a["w_out"][i][order]
        for m in range(KD):
            put(f"out{m}", _chunk(wo[:, P * m:P * (m + 1)]))
            put(f"gate{m}", _chunk(a["ple_gate"][i][:, P * m:P * (m + 1)]))
        for half in range(2):
            put(f"proj{half}", np.concatenate(
                [_chunk(a["ple_proj"][i][:, P * m:P * (m + 1)]) for m in range(4 * half, 4 * half + 4)], axis=1))
    return out


def _rows(v):
    return v.reshape(-1, P).T


def _constants():
    half = ROPE // 2
    inv = np.exp(np.float32(-np.log(10000.0)) * np.arange(half, dtype=np.float32) / np.float32(half)) \
        .astype(np.float32)
    ang = np.arange(TOK, dtype=np.float32)[None, :] * inv[:, None]
    cos, sin = np.cos(ang).astype(np.float32), np.sin(ang).astype(np.float32)
    cos_sin = np.concatenate([cos, cos, -sin, sin] * 2, axis=0)
    comb = np.zeros((P, 3, 96), np.float32)
    for i in range(ROPE):
        for a, first in ((0, 0), (1, 0), (2, 64)):
            comb[first + i, a, 64 + i] = comb[first + 32 + i, a, 64 + i] = 1
    head_ones = np.kron(np.eye(2), np.full((64, 64), 1 / 64)).astype(np.float32)
    q, k = np.arange(P)[:, None], np.arange(256)[None, :]
    back = (q + 128) // 64 - k // 64
    dist = np.where((back >= 0) & (back <= 2), np.abs(q + 128 - k), FAR).astype(np.float32)
    s, t = np.arange(P)[:, None], np.arange(P)[None, :]
    mask = np.zeros((P, LEVELS - 1, P), np.float32)
    for lv in range(1, LEVELS):
        m = 1 << lv
        mask[:, lv - 1] = (s // m == t // m) & (s % m < m // 2) & (t % m >= m // 2)
    late = np.zeros((1, P + 64), np.float32)
    late[0, :64] = 1
    late[0, P:] = NEG
    return dict(cos_sin=cos_sin, ident_d=np.eye(P, dtype=np.float32),
                ones_d=np.full((P, P), 1 / D_MODEL, np.float32), head_ones_d=head_ones, comb_d=comb,
                dist_d=dist, mask_d=mask, late_d=late)


def kernel(**inputs):
    import concourse.bacc as bacc
    from concourse.bass_utils import run_bass_kernel_spmd

    a = {k: np.asarray(v) for k, v in inputs.items()}

    def tokens(prompt, sample):
        both = np.concatenate([prompt, sample], axis=0).T
        return both.reshape(-1, P, TOK).transpose(1, 0, 2)

    par = np.zeros((DEPTH + 1, P, PAR_W), np.float32)
    par[DEPTH, :, PAR["next"]:PAR["next"] + KD] = _rows(a["ffn1_norm"][0])
    uq = np.zeros((DEPTH, P, 2, 3, 256), np.float32)
    ukv = np.zeros((DEPTH, P, 3, 256), np.float32)
    for i in range(DEPTH):
        following = a["ffn1_norm"][i + 1] if i + 1 < DEPTH else a["final_norm"]
        for key, v in (("mix", a["mix_norm"][i]), ("ffn2", a["ffn2_norm"][i]), ("ple", a["ple_norm"][i]),
                       ("next", following), ("q_norm", a["mla_q_norm"][i]), ("kv_norm", a["mla_kv_norm"][i]),
                       ("hg_out", np.concatenate([a["hg_out_norm"][i]] * 2))):
            par[i, :, PAR[key]:PAR[key] + v.size // P] = _rows(v)
        par[i, :, PAR["sink"]:PAR["sink"] + 6] = a["swa_sinks"][i][None, :]
        wq = a["mla_w_uq"][i].reshape(2, P, 6, 96).transpose(1, 0, 2, 3)
        wkv = a["mla_w_ukv"][i].reshape(P, 6, 128)
        for pr in range(3):
            for e in range(2):
                hd = wq[:, :, 2 * pr + e]
                rot = hd[:, :, 64:]
                uq[i, :, :, pr, 64 * e:64 * e + 32] = rot
                uq[i, :, :, pr, 64 * e + 32:64 * e + 64] = np.concatenate([rot[..., 16:], rot[..., :16]], axis=-1)
                uq[i, :, :, pr, 128 + 64 * e:192 + 64 * e] = hd[:, :, :64]
                ukv[i, :, pr, 64 * e:64 * e + 64] = wkv[:, 2 * pr + e, :64]
                ukv[i, :, pr, 128 + 64 * e:192 + 64 * e] = wkv[:, 2 * pr + e, 64:]

    c = _constants()
    feed = dict(
        x_t=tokens(a["x_prompt"][0], a["x_sample"][0]),
        p_t=np.stack([tokens(a["p_prompt"][i, 0], a["p_sample"][i, 0]) for i in range(DEPTH)]),
        w_all=_weights(a), uq=uq, ukv=ukv, par_d=par,
        logits_d=np.stack([_rows(a["hg_lb_logits"][i]) for i in range(DEPTH)], axis=1),
        cos_sin=c["cos_sin"], ident_d=c["ident_d"], ones_d=c["ones_d"], head_ones_d=c["head_ones_d"],
        comb_d=c["comb_d"], dist_d=c["dist_d"], mask_d=c["mask_d"], late_d=c["late_d"],
        ckv_c=a["cache_mla_ckv"][:, 0].transpose(0, 2, 1), krope_c=a["cache_mla_krope"][:, 0].transpose(0, 2, 1),
        swk_c=a["cache_swa_k"][:, 0].reshape(DEPTH, 128, 128).transpose(0, 2, 1),
        swv_c=a["cache_swa_v"][:, 0].reshape(DEPTH, 128, 128),
        hg_s=a["state_hgrn"][:, 0].reshape(DEPTH, 2, P, 64).transpose(0, 2, 1, 3),
    )
    outs = dict(y_t=(P, KD, TOK), ckv_o=(DEPTH, P, TOK), krope_o=(DEPTH, ROPE, TOK),
                swk_o=(DEPTH, 2, P, P), swv_o=(DEPTH, 2, P, P), hg_o=(DEPTH, 2, P, 2, 64))
    nc = bacc.Bacc("TRN2", target_bir_lowering=False, num_devices=1)
    feed = {k: np.ascontiguousarray(v) for k, v in feed.items()}
    args = {k: nc.dram_tensor(k, v.shape, mybir.dt.from_np(v.dtype), kind="ExternalInput").ap()
            for k, v in feed.items()}
    args |= {k: nc.dram_tensor(k, s, F32, kind="ExternalOutput").ap() for k, s in outs.items()}
    hybrid_step(nc, **args)
    res = run_bass_kernel_spmd(nc, [feed], core_ids=[0]).results[0]

    y = res["y_t"].transpose(2, 1, 0).reshape(TOK, D_MODEL)
    ckv = res["ckv_o"].transpose(0, 2, 1)
    krope = res["krope_o"].transpose(0, 2, 1)
    swk = res["swk_o"].transpose(0, 1, 3, 2).reshape(DEPTH, 2, 1, 128, 2, 64)
    swv = res["swv_o"].reshape(DEPTH, 2, 1, 128, 2, 64)
    hgs = res["hg_o"].transpose(0, 1, 3, 2, 4).reshape(DEPTH, 2, 1, 4, 64, 64)
    c = np.ascontiguousarray
    return (c(y[None, :PROMPT]), c(y[None, PROMPT:]),
            c(ckv[:, None, :PROMPT]), c(krope[:, None, :PROMPT]), c(swk[:, 0]), c(swv[:, 0]), c(hgs[:, 0]),
            c(ckv[:, None, PROMPT:]), c(krope[:, None, PROMPT:]), c(swk[:, 1]), c(swv[:, 1]), c(hgs[:, 1]))
```
